# Optimizing a Trainium2 kernel written in Bass

```python
import jax, jax.numpy as jnp
from jax import lax
import numpy as np

D_MODEL = 1024
BATCH = 1
SEQ = 512
DEPTH = 1

CHUNK = 64
EPS = 1e-6
GMLP_BLOCK = 128
GMLP_GROUPS = 4
GMLP_GROUP_DIM = 128
GMLP_WIDTH = GMLP_GROUPS * GMLP_GROUP_DIM
HG_HEADS = 8
HG_DK = 128
HG_DV = D_MODEL // HG_HEADS
HG_WIDTH = HG_HEADS * HG_DK
HG_VWIDTH = HG_HEADS * HG_DV
N_BRANCH = 2
D_FF = 4 * D_MODEL
IN_SPLITS = (GMLP_WIDTH, GMLP_WIDTH, HG_WIDTH, HG_WIDTH, HG_VWIDTH, HG_VWIDTH, D_MODEL, D_MODEL)
IN_COLS = sum(IN_SPLITS)


def rmsnorm(x, g):
    xf = x.astype(jnp.float32)
    y = xf * lax.rsqrt(jnp.mean(xf * xf, axis=-1, keepdims=True) + EPS)
    return (y * g.astype(jnp.float32)).astype(x.dtype)

def layernorm(x, g, b):
    xf = x.astype(jnp.float32)
    mu = jnp.mean(xf, axis=-1, keepdims=True)
    xc = xf - mu
    y = xc * lax.rsqrt(jnp.mean(xc * xc, axis=-1, keepdims=True) + EPS)
    return (y * g.astype(jnp.float32) + b.astype(jnp.float32)).astype(x.dtype)

def chunk_causal_mask(n):
    c = jnp.arange(n) // CHUNK
    return c[None, :] <= c[:, None]

def gmlp_branch(zu, zv, ln_g, ln_b, w_s, b_s):
    B, S, _ = zu.shape
    nb = S // GMLP_BLOCK
    u = jax.nn.gelu(zu, approximate=False)
    v = layernorm(jax.nn.gelu(zv, approximate=False), ln_g, ln_b)
    v = v.reshape(B, nb, GMLP_BLOCK, GMLP_GROUPS, GMLP_GROUP_DIM)
    w = jnp.where(chunk_causal_mask(GMLP_BLOCK)[None], w_s, 0).astype(v.dtype)
    mixed = jnp.einsum('gqp,bnpgc->bnqgc', w, v) + b_s.T.astype(v.dtype)[None, None, :, :, None]
    return u * mixed.reshape(B, S, GMLP_WIDTH)

def hgrn2_lower_bounds(lb_param):
    p = jax.nn.softmax(lb_param.astype(jnp.float32), axis=0)
    return jnp.cumsum(p, axis=0) - p[0]

def hgrn2_chunkwise(q, k, v, log_f):
    B, S, H, DK = q.shape
    DV = v.shape[-1]
    nc = S // CHUNK

    def to_chunks(t):
        return t.reshape(B, nc, CHUNK, H, t.shape[-1]).transpose(1, 0, 3, 2, 4)

    tri = jnp.tril(jnp.ones((CHUNK, CHUNK), dtype=bool))[:, :, None]

    def step(state, inp):
        qb, kb, vb, gb = inp
        cum = jnp.cumsum(gb, axis=2)
        o_inter = jnp.einsum('bhtk,bhkv->bhtv', qb * jnp.exp(cum), state)
        rel = cum[:, :, :, None, :] - cum[:, :, None, :, :]
        decay = jnp.exp(jnp.where(tri, rel, -jnp.inf))
        scores = jnp.einsum('bhtk,bhsk,bhtsk->bhts', qb, kb, decay)
        o_intra = jnp.einsum('bhts,bhsv->bhtv', scores, vb)
        last = cum[:, :, -1:, :]
        k_dec = kb * jnp.exp(last - cum)
        state = state * jnp.exp(last[:, :, 0, :])[..., None] + jnp.einsum('bhsk,bhsv->bhkv', k_dec, vb)
        return state, o_inter + o_intra

    state0 = jnp.zeros((B, H, DK, DV), jnp.float32)
    _, out = lax.scan(step, state0, (to_chunks(q), to_chunks(k), to_chunks(v), to_chunks(log_f)))
    return out.transpose(1, 0, 3, 2, 4).reshape(B, S, H, DV)

def hgrn2_branch(zq, zf, zi, zo, lb, layer_idx, norm_g):
    B, S, _ = zq.shape
    dt = zq.dtype
    zf32 = zf.astype(jnp.float32)
    if layer_idx == 0:
        log_f = jax.nn.log_sigmoid(zf32)
        k = jax.nn.sigmoid(-zf32)
    else:
        f = lb[None, None, :] + (1.0 - lb[None, None, :]) * jax.nn.sigmoid(zf32)
        log_f = jnp.log(f)
        k = 1.0 - f
    q = jax.nn.silu(zq.astype(jnp.float32))
    heads = lambda t, d: t.reshape(B, S, HG_HEADS, d)
    o = hgrn2_chunkwise(heads(q, HG_DK), heads(k, HG_DK),
                        heads(zi.astype(jnp.float32), HG_DV), heads(log_f, HG_DK))
    o = rmsnorm(o, norm_g) * jax.nn.silu(heads(zo.astype(jnp.float32), HG_DV))
    return o.reshape(B, S, HG_VWIDTH).astype(dt)

def first_inputs(seed: int = 0) -> dict:
    key = jax.random.key(seed)
    ks = jax.random.split(key, 16)
    n = jax.random.normal
    f32 = jnp.float32
    return {
        "x": n(ks[0], (BATCH, SEQ, D_MODEL), f32),
        "w_in": n(ks[1], (DEPTH, D_MODEL, IN_COLS), f32) * D_MODEL ** -0.5,
        "gmlp_ln_g": 1.0 + 0.05 * n(ks[2], (DEPTH, GMLP_WIDTH), f32),
        "gmlp_ln_b": 0.02 * n(ks[3], (DEPTH, GMLP_WIDTH), f32),
        "gmlp_ws": n(ks[4], (DEPTH, GMLP_GROUPS, GMLP_BLOCK, GMLP_BLOCK), f32) * GMLP_BLOCK ** -0.5,
        "gmlp_bs": 1.0 + 0.05 * n(ks[5], (DEPTH, GMLP_GROUPS, GMLP_BLOCK), f32),
        "w_up_a": n(ks[6], (DEPTH, GMLP_WIDTH, D_MODEL), f32) * GMLP_WIDTH ** -0.5,
        "hg_lb": 0.5 * n(ks[7], (DEPTH, HG_WIDTH), f32),
        "hg_norm_g": 1.0 + 0.05 * n(ks[8], (DEPTH, HG_DV), f32),
        "w_up_b": n(ks[9], (DEPTH, HG_VWIDTH, D_MODEL), f32) * HG_VWIDTH ** -0.5,
        "w_out": n(ks[10], (DEPTH, D_MODEL, D_MODEL), f32) * D_MODEL ** -0.5,
        "norm_mix": 1.0 + 0.05 * n(ks[11], (DEPTH, D_MODEL), f32),
        "norm_ffn": 1.0 + 0.05 * n(ks[12], (DEPTH, D_MODEL), f32),
        "w_ff1": n(ks[13], (DEPTH, D_MODEL, D_FF), f32) * D_MODEL ** -0.5,
        "w_ff2": n(ks[14], (DEPTH, D_FF, D_MODEL), f32) * (0.5 * D_FF ** -0.5),
        "final_norm": 1.0 + 0.05 * n(ks[15], (D_MODEL,), f32),
    }

def first_block(x, w_in, gmlp_ln_g, gmlp_ln_b, gmlp_ws, gmlp_bs, w_up_a, hg_lb, hg_norm_g,
              w_up_b, w_out, norm_mix, norm_ffn, w_ff1, w_ff2, final_norm):
    split_points = [int(s) for s in np.cumsum(IN_SPLITS)[:-1]]
    lower_bounds = hgrn2_lower_bounds(hg_lb)
    for l in range(DEPTH):
        h = rmsnorm(x, norm_mix[l])
        proj = h @ w_in[l]
        zu, zv, zq, zf, zi, zo, g_a, g_b = jnp.split(proj, split_points, axis=-1)
        y_a = gmlp_branch(zu, zv, gmlp_ln_g[l], gmlp_ln_b[l], gmlp_ws[l], gmlp_bs[l]) @ w_up_a[l]
        y_b = hgrn2_branch(zq, zf, zi, zo, lower_bounds[l], l, hg_norm_g[l]) @ w_up_b[l]
        mix = jax.nn.sigmoid(g_a) * y_a + jax.nn.sigmoid(g_b) * y_b
        x = x + mix @ w_out[l]
        h = rmsnorm(x, norm_ffn[l])
        x = x + jnp.square(jax.nn.relu(h @ w_ff1[l])) @ w_ff2[l]
    return rmsnorm(x, final_norm)


DEPTH_2 = 2

N_A = DEPTH_2 // 2
N_B = DEPTH_2 - N_A
N_HEADS = 16
HEAD_DIM = D_MODEL // N_HEADS
CONV_W = 3
D_FF_2 = 2816
Q_BLOCK = 128


def rmsnorm_2(x, g):
    xf = x.astype(jnp.float32)
    y = xf * lax.rsqrt(jnp.mean(xf * xf, axis=-1, keepdims=True) + EPS)
    return (y * g).astype(x.dtype)

def causal_dwconv(u, w):
    width = w.shape[0]
    s = u.shape[1]
    up = jnp.pad(u, ((0, 0), (width - 1, 0), (0, 0)))
    return sum(up[:, i:i + s] * w[i] for i in range(width))

def short_conv_mixer(xn, w_in, conv_w, w_out):
    proj = xn @ w_in
    b, c, h = jnp.split(proj, 3, axis=-1)
    u = causal_dwconv(c * h, conv_w)
    return (b * u) @ w_out

def conv_ffn(xn, w_up, conv_w, w_down):
    up = xn @ w_up
    a, g = jnp.split(up, 2, axis=-1)
    a = causal_dwconv(a, conv_w)
    return (jax.nn.silu(a) * g) @ w_down

def forgetting_attention(q, k, v, c):
    bsz, nh, s_len, hd = q.shape
    nb = s_len // Q_BLOCK
    scale = hd ** -0.5
    qb = q.reshape(bsz, nh, nb, Q_BLOCK, hd).transpose(2, 0, 1, 3, 4)
    cb = c.reshape(bsz, nh, nb, Q_BLOCK).transpose(2, 0, 1, 3)
    kpos = jnp.arange(s_len)

    def one_block(args):
        q_i, c_i, i = args
        s = jnp.einsum('bhqd,bhkd->bhqk', q_i, k, preferred_element_type=jnp.float32) * scale
        s = s + c_i[..., None] - c[:, :, None, :]
        qpos = i * Q_BLOCK + jnp.arange(Q_BLOCK)
        s = jnp.where(kpos[None, :] <= qpos[:, None], s, -jnp.inf)
        p = jax.nn.softmax(s, axis=-1)
        return jnp.einsum('bhqk,bhkd->bhqd', p.astype(v.dtype), v)

    o = lax.map(one_block, (qb, cb, jnp.arange(nb)))
    return o.transpose(1, 0, 3, 2, 4).reshape(bsz, s_len, nh * hd)

def second_inputs(seed: int = 0) -> dict:
    key = jax.random.key(seed)
    ks = jax.random.split(key, 17)
    f32 = jnp.float32
    out_scale = (2 * DEPTH_2) ** -0.5

    def nrm(k, shape, scale):
        return jax.random.normal(k, shape, f32) * scale

    def gain(k, shape):
        return 1.0 + 0.02 * jax.random.normal(k, shape, f32)

    x = nrm(ks[0], (BATCH, SEQ, D_MODEL), 1.0)
    attn_norm = gain(ks[1], (DEPTH_2, D_MODEL))
    ffn_norm = gain(ks[2], (DEPTH_2, D_MODEL))
    a_w_in = nrm(ks[3], (N_A, D_MODEL, 3 * D_MODEL), D_MODEL ** -0.5)
    a_conv = nrm(ks[4], (N_A, CONV_W, D_MODEL), CONV_W ** -0.5)
    a_w_out = nrm(ks[5], (N_A, D_MODEL, D_MODEL), out_scale * D_MODEL ** -0.5)
    kv_norm = gain(ks[6], (D_MODEL,))
    w_kvf = jnp.concatenate([
        nrm(ks[7], (D_MODEL, 2 * D_MODEL), D_MODEL ** -0.5),
        nrm(ks[8], (D_MODEL, N_HEADS), 0.1 * D_MODEL ** -0.5),
    ], axis=1)
    b_f = jax.random.uniform(ks[9], (N_HEADS,), f32, 1.0, 6.0)
    k_norm = gain(ks[10], (HEAD_DIM,))
    b_w_qg = nrm(ks[11], (N_B, D_MODEL, 2 * D_MODEL), D_MODEL ** -0.5)
    q_norm = gain(ks[12], (N_B, HEAD_DIM))
    b_w_out = nrm(ks[13], (N_B, D_MODEL, D_MODEL), out_scale * D_MODEL ** -0.5)
    ffn_w_up = nrm(ks[14], (DEPTH_2, D_MODEL, 2 * D_FF_2), D_MODEL ** -0.5)
    ffn_conv = nrm(ks[15], (DEPTH_2, CONV_W, D_FF_2), CONV_W ** -0.5)
    ffn_w_down = nrm(ks[16], (DEPTH_2, D_FF_2, D_MODEL), out_scale * D_FF_2 ** -0.5)
    return {"x": x, "attn_norm": attn_norm, "ffn_norm": ffn_norm,
            "a_w_in": a_w_in, "a_conv": a_conv, "a_w_out": a_w_out,
            "kv_norm": kv_norm, "w_kvf": w_kvf, "b_f": b_f, "k_norm": k_norm,
            "b_w_qg": b_w_qg, "q_norm": q_norm, "b_w_out": b_w_out,
            "ffn_w_up": ffn_w_up, "ffn_conv": ffn_conv, "ffn_w_down": ffn_w_down}

def second_block(x, attn_norm, ffn_norm, a_w_in, a_conv, a_w_out, kv_norm, w_kvf, b_f,
              k_norm, b_w_qg, q_norm, b_w_out, ffn_w_up, ffn_conv, ffn_w_down):
    bsz, s_len, d = x.shape
    k = v = c = None
    for l in range(DEPTH_2):
        if l < N_A:
            xn = rmsnorm_2(x, attn_norm[l])
            x = x + short_conv_mixer(xn, a_w_in[l], a_conv[l], a_w_out[l])
        else:
            if l == N_A:
                h = rmsnorm_2(x, kv_norm)
                kvf = h @ w_kvf
                k_s = kvf[..., :d].reshape(bsz, s_len, N_HEADS, HEAD_DIM)
                v_s = kvf[..., d:2 * d].reshape(bsz, s_len, N_HEADS, HEAD_DIM)
                f_logit = (kvf[..., 2 * d:] + b_f).astype(jnp.float32)
                k = rmsnorm_2(k_s, k_norm).transpose(0, 2, 1, 3)
                v = v_s.transpose(0, 2, 1, 3)
                c = jnp.cumsum(jax.nn.log_sigmoid(f_logit), axis=1).transpose(0, 2, 1)
            j = l - N_A
            xn = rmsnorm_2(x, attn_norm[l])
            qg = xn @ b_w_qg[j]
            q = rmsnorm_2(qg[..., :d].reshape(bsz, s_len, N_HEADS, HEAD_DIM), q_norm[j])
            q = q.transpose(0, 2, 1, 3)
            o = forgetting_attention(q, k, v, c)
            o = o * jax.nn.sigmoid(qg[..., d:])
            x = x + o @ b_w_out[j]
        xn = rmsnorm_2(x, ffn_norm[l])
        x = x + conv_ffn(xn, ffn_w_up[l], ffn_conv[l], ffn_w_down[l])
    return x


def setup_inputs(seed=0):
    out = dict(first_inputs(seed))
    for name, value in second_inputs(seed + 1).items():
        if name != "x":
            out[name + "_2"] = value
    return out


def reference(
    x, w_in, gmlp_ln_g, gmlp_ln_b, gmlp_ws, gmlp_bs, w_up_a, hg_lb, hg_norm_g, w_up_b, w_out,
    norm_mix, norm_ffn, w_ff1, w_ff2, final_norm, attn_norm_2, ffn_norm_2, a_w_in_2, a_conv_2,
    a_w_out_2, kv_norm_2, w_kvf_2, b_f_2, k_norm_2, b_w_qg_2, q_norm_2, b_w_out_2, ffn_w_up_2,
    ffn_conv_2, ffn_w_down_2,
):
    x = first_block(
        x, w_in, gmlp_ln_g, gmlp_ln_b, gmlp_ws, gmlp_bs, w_up_a, hg_lb, hg_norm_g, w_up_b,
        w_out, norm_mix, norm_ffn, w_ff1, w_ff2, final_norm,
    )
    return second_block(
        x, attn_norm_2, ffn_norm_2, a_w_in_2, a_conv_2, a_w_out_2, kv_norm_2, w_kvf_2, b_f_2,
        k_norm_2, b_w_qg_2, q_norm_2, b_w_out_2, ffn_w_up_2, ffn_conv_2, ffn_w_down_2,
    )


_drawn_inputs = setup_inputs


def setup_inputs(seed=0):
    import zlib

    import numpy as np

    out = dict(_drawn_inputs(seed))
    spreads = {}
    factors = {'gmlp_ln_g': 3.265,
     'gmlp_ln_b': 8.0,
     'gmlp_bs': 2.757,
     'hg_norm_g': 2.942,
     'attn_norm_2': 3.383,
     'ffn_norm_2': 5.384,
     'kv_norm_2': 28.985,
     'k_norm_2': 31.997,
     'q_norm_2': 27.439}
    for name, (base, spread) in spreads.items():
        noise = np.random.default_rng([zlib.crc32(name.encode()), seed]).standard_normal(out[name].shape)
        drawn = base * np.exp(spread * noise) if base else spread * noise
        out[name] = __import__('jax').numpy.asarray(drawn.astype(out[name].dtype))
    for name, factor in factors.items():
        out[name] = (out[name] * factor).astype(out[name].dtype)
    return out
```

```python
from contextlib import ExitStack, contextmanager

import numpy as np

import concourse.bass as bass
from concourse import mybir

P = 128
SEQ = 512
D = 1024
DT = D // P
GROUPS = 4
HEADS_H = 8
D_FF1 = 4 * D
FF1_CHUNKS = D_FF1 // D
D_FF2 = 2816
FF2_TILES = D_FF2 // P
FF2_CHUNKS = (8, 8, 6)
HEADS_A = 16
HEAD_DIM = 64
EPS = 1e-6
BLK = SEQ // P
HALVES = (64, 32, 16, 8, 4, 2, 1)
LEVELS = len(HALVES)
NEG = -1e30
ARENA = 16916

RING = 4
COUNTS = [("zu", 4), ("zv", 4), ("ga", 8), ("upa", 8), ("heads", 32), ("gb", 8), ("upb", 8), ("out1", 8),
          ("ff1", 64), ("conv_b", 8), ("conv_ch", 16), ("out2", 8), ("ffn_0", 68), ("k", 8), ("v", 8),
          ("f", 1), ("qg", 16), ("out3", 8), ("ffn_1", 68)]
START, N_PANELS = {}, 0
for _name, _n in COUNTS:
    START[_name] = N_PANELS
    N_PANELS += _n

CONST_COLS, PARAM_COLS = {}, {}
_at = 0
for _name, _n in [("ident", P), ("ones", P), ("halves", P), ("minus", P), ("neg", P), ("reset", SEQ),
                  ("levels", LEVELS * P), ("onehot", HEADS_A)]:
    CONST_COLS[_name] = (_at, _n)
    _at += _n
N_CONST = _at
_at = 0
for _name, _n in [("norm_mix", DT), ("norm_ffn", DT), ("final_norm", DT), ("attn_0", DT), ("attn_1", DT),
                  ("ffn_0", DT), ("ffn_1", DT), ("kv", DT), ("hg_norm", 1), ("k_norm", 1), ("q_norm", 1),
                  ("b_f", 1), ("a_conv", 3 * DT), ("conv_0", 3 * FF2_TILES), ("conv_1", 3 * FF2_TILES)]:
    PARAM_COLS[_name] = (_at, _n)
    _at += _n
N_PARAM = _at

R_MIX, R_HEAD, R_FFN, R_FINAL, R_ATTN0, R_FFN0, R_ATTN1, R_K, R_Q, R_FFN1 = 0, 1, 9, 10, 11, 12, 13, 14, 22, 30
S_MIX, S_FFN, S_FINAL, S_ATTN0, S_FFN0, S_ATTN1, S_FFN1 = range(7)
X_MIX, X_FFN, X_ATTN0, X_FFN0, X_KV, X_Q, X_FFN1 = range(7)
HID_GMLP, HID_HEADS, HID_MIX, HID_FF1, HID_CONV, HID_FFN0, HID_ATTN, HID_FFN1 = 0, 4, 12, 20, 52, 60, 82, 90


class Steps:

    def __init__(self, eng, sem):
        self.eng, self.sem, self.n, self.offset = eng, sem, 0, 0

    def done(self, ins):
        ins.then_inc(self.sem, 1)
        self.n += 1
        return ins

    def wait(self):
        self.eng.wait_ge(self.sem, self.n + self.offset)

    @contextmanager
    def loop(self, first, end, marks):
        before = self.n
        with self.eng.Fori(first, end) as i:
            self.offset = (i - first) * marks
            yield i
        self.offset = 0
        assert self.n - before == marks, f"the body marks {self.n - before} steps, not {marks}"
        self.n = before + (end - first) * marks


def tile_at(buf, i):
    if isinstance(i, int):
        return buf[:, i, :]
    return buf[:, bass.ds(i, 1), :].rearrange("p a n -> p (a n)")


def column(buf, i, rows=P):
    return buf[0:rows, i:i + 1] if isinstance(i, int) else buf[0:rows, bass.ds(i, 1)]


def build(nc, xT, panels, const, param, rows, ws, outT):
    F, R, BF = mybir.dt.float32, mybir.dt.float32r, mybir.dt.bfloat16
    ALU = mybir.AluOpType
    ACT = mybir.ActivationFunctionType

    ctx = ExitStack()
    with ctx:
        def sb(name, shape, dt=F):
            return ctx.enter_context(nc.sbuf_tensor(name, shape, dt))

        def sem(name):
            return ctx.enter_context(nc.semaphore(name))

        w_raw = sb("w_raw", [P, RING, D])
        w_hi = sb("w_hi", [P, RING, D], R)
        w_lo = sb("w_lo", [P, RING, D], R)
        x = sb("x", [P, DT, SEQ])
        x_hi = sb("x_hi", [P, DT, SEQ], R)
        x_lo = sb("x_lo", [P, DT, SEQ], R)
        hid_hi = sb("hid_hi", [P, DT, SEQ], R)
        hid_lo = sb("hid_lo", [P, DT, SEQ], R)
        consts = sb("consts", [P, N_CONST])
        params = sb("params", [P, N_PARAM])
        identb = sb("identb", [P, P], BF)
        negb = sb("negb", [P, P], BF)
        wait_mark = sb("wait_mark", [P, 1])
        inv_rms = sb("inv_rms", [P, SEQ])
        var = sb("var", [P, SEQ])
        arena = sb("arena", [P, ARENA])

        def c(name):
            a, n = CONST_COLS[name]
            return consts[:, a:a + n]

        def gain(name, i=0):
            a, _ = PARAM_COLS[name]
            return column(params, a + i)

        used = [0]

        def take(*shape):
            n = int(np.prod(shape))
            a = used[0]
            used[0] += n
            assert used[0] <= ARENA, used[0]
            v = arena[:, a:a + n]
            if len(shape) == 2:
                v = v.rearrange("p (a n) -> p a n", a=shape[0])
            return v

        squares = take(2, SEQ)
        sum_sq = take(SEQ)
        o_sq, o_inv, o_tmp = squares[:, 0, :], squares[:, 1, :], sum_sq
        common = used[0]
        y = take(DT, SEQ)
        after_y = used[0]
        zu, zv = take(GROUPS, SEQ), take(GROUPS, SEQ)
        vn = take(BLK, SEQ)
        rows_sb = take(3, SEQ)
        ws_sb = take(GROUPS, P)
        ln_stats, ln_mv = take(BLK, 6), take(BLK, 2)
        ln_root, ln_inv = take(BLK), take(BLK)
        used[0] = after_y
        qk = take(2 + LEVELS, SEQ)
        masked = take(LEVELS + 1, P)
        z, za, g, cum = take(SEQ), take(SEQ), take(SEQ), take(SEQ)
        q, k, vT, silu_o = take(SEQ), take(SEQ), take(SEQ), take(SEQ)
        v_nat, k_nat, scores = take(BLK, P), take(BLK - 1, P), take(BLK, P)
        state = k_nat
        chunk_decay = take(BLK)
        used[0] = after_y
        gb = take(DT, SEQ)
        gy = take(2, SEQ)
        used[0] = after_y
        relu = take(2, SEQ)
        relu_sq = take(2, SEQ)
        used[0] = common
        conv_b = take(DT, SEQ)
        padded = take(2, SEQ + 2)
        conv_c, conv_t, conv_u, conv_o = take(2, SEQ), take(2, SEQ), take(2, SEQ), take(2, SEQ)
        used[0] = common
        k_all, v_all = take(DT, SEQ), take(DT, SEQ)
        attn_common = used[0]
        k_raw, v_raw, k_sq = take(2, SEQ), take(2, SEQ), take(2, SEQ)
        k_inv = take(SEQ)
        used[0] = attn_common
        OFF_P = [0, 128, 384, 768]
        OFF_T = [0, 512, 896, 1152]
        prob, prob_t = take(1280), take(1280)
        gate = take(2, SEQ)
        q_raw, q_n, q_sq = take(SEQ), take(SEQ), take(SEQ)
        q_inv = q_sq
        k_now, v_now, key_bias, o_all = take(SEQ), take(SEQ), take(SEQ), take(SEQ)
        log_c, log_pick = squares[:, 0, :], squares[:, 1, :]
        logit, logit_a = prob[:, 0:SEQ], prob[:, SEQ:2 * SEQ]
        row_max, row_neg, row_sum, row_inv = take(BLK), take(BLK), take(BLK), take(BLK)

        ps = ctx.enter_context(nc.psum_tensor("ps", [P, 8, SEQ], F))

        w_in = [sem(f"w_in{i}") for i in range(RING)]
        w_high, w_low = sem("w_high"), sem("w_low")
        made = sem("made")
        evicted = sem("evicted")
        x_in, c_in, row_in, out_done = sem("x_in"), sem("c_in"), sem("row_in"), sem("out_done")
        consts_ok = sem("consts_ok")
        x_high, x_low = sem("x_high"), sem("x_low")
        hid_high, hid_low = sem("hid_high"), sem("hid_low")
        squared, summed = sem("squared"), sem("summed")
        sums_ready, var_ready, root_ready = sem("sums_ready"), sem("var_ready"), sem("root_ready")
        x_final = sem("x_final")
        dve_steps, act_steps, pool_steps = sem("dve_steps"), sem("act_steps"), sem("pool_steps")
        gelu_done, v_turned, ln_var, ln_rooted, v_normed = (sem(n) for n in (
            "gelu_done", "v_turned", "ln_var", "ln_rooted", "v_normed"))
        mixed, mixed_read, y_a, ws_masked = sem("mixed"), sem("mixed_read"), sem("y_a"), sem("ws_masked")
        gate_a, gate_b, y_mixed = sem("gate_a"), sem("gate_b"), sem("y_mixed")
        f_abs, f_log, f_k, k_done, q_exp, q_done, i_done, o_exp, o_gate = (sem(n) for n in (
            "f_abs", "f_log", "f_k", "k_done", "q_exp", "q_done", "i_done", "o_exp", "o_gate"))
        turned_v, turned_k, diag_made, copied_v, copied_k, diag_kept = (sem(n) for n in (
            "turned_v", "turned_k", "diag_made", "copied_v", "copied_k", "diag_kept"))
        level_made, level_masked, scores_done, kv_made, states_done = (sem(n) for n in (
            "level_made", "level_masked", "scores_done", "kv_made", "states_done"))
        spans_done, decays_done, keys_decayed, queries_decayed = (sem(n) for n in (
            "spans_done", "decays_done", "keys_decayed", "queries_decayed"))
        o_made, o_squared, y_b, cum_done = sem("o_made"), sem("o_squared"), sem("y_b"), sem("cum_done")
        relu_done, conv_done, silu_done, hid_raw = (sem(n) for n in (
            "relu_done", "conv_done", "silu_done", "hid_raw"))
        k_squared, k_normed, v_copied, v_flat, v_spread = (sem(n) for n in (
            "k_squared", "k_normed", "v_copied", "v_flat", "v_spread"))
        l_abs, l_log, l_done, picked, biased, bias_read = (sem(n) for n in (
            "l_abs", "l_log", "l_done", "picked", "biased", "bias_read"))
        head_loaded, scored, maxed, exped, scaled, turned_p, copied_even, copied_odd, attended, attn_read = (sem(n) for n in (
            "head_loaded", "scored", "maxed", "exped", "scaled", "turned_p", "copied_even", "copied_odd", "attended", "attn_read"))
        q_squared, q_normed, gate_g = sem("q_squared"), sem("q_normed"), sem("gate_g")

        block = ctx.enter_context(nc.Block())

        S = START

        @block.sync
        def _(sp):
            def load(i, j):
                sp.dma_start(w_raw[:, j, :], panels[bass.ds(i * RING + j, 1)].rearrange("a p n -> p (a n)")
                             if not isinstance(i, int) else panels[i * RING + j]).then_inc(w_in[j], 16)

            sp.dma_start(consts[:], const).then_inc(c_in, 16)
            sp.dma_start(params[:], param).then_inc(c_in, 16)
            for m in range(DT):
                sp.dma_start(x[:, m, :], xT[m]).then_inc(x_in, 16)
            for j in range(RING):
                load(0, j)
            sp.dma_start(rows_sb[:, :, :], rows.partition_broadcast(P)).then_inc(row_in, 16)
            sp.dma_start(ws_sb[:, :, :], ws).then_inc(row_in, 16)
            with sp.Fori(1, N_PANELS // RING) as i:
                at = sp.snap(i * RING)
                for j in range(RING):
                    src = panels[bass.ds(at + j, 1)].rearrange("a p n -> p (a n)")
                    sp.wait_ge(w_low, i * RING + (j - RING + 1))
                    sp.dma_start(w_raw[:, j, :], src).then_inc(w_in[j], 16)
            for pnl in range(N_PANELS - N_PANELS % RING, N_PANELS):
                sp.wait_ge(w_low, pnl - RING + 1)
                sp.dma_start(w_raw[:, pnl % RING, :], panels[pnl]).then_inc(w_in[pnl % RING], 16)
            for m in range(DT):
                sp.wait_ge(evicted, N_PANELS - DT + m + 1)
                sp.dma_start(outT[m], x[:, m, :]).then_inc(out_done, 16)
            sp.wait_ge(out_done, 16 * DT)

        @block.gpsimd
        def _(pool):
            steps = Steps(pool, pool_steps)

            def low(p, j):
                if isinstance(p, int) and p >= N_PANELS:
                    return
                pool.wait_ge(w_high, p + 1)
                if not isinstance(p, int) or p >= RING:
                    pool.wait_ge(made, p - RING + 1)
                nc.gpsimd.tensor_tensor(w_lo[:, j, :], w_raw[:, j, :], w_hi[:, j, :].bitcast(F),
                                        ALU.subtract).then_inc(w_low, 1)

            first = S["heads"] + 3
            for p in range(RING):
                low(p, p)
            with pool.Fori(1, first // RING) as i:
                for j in range(RING):
                    low(i * RING + j, j)
            for p in range(first - first % RING, first):
                low(p, p % RING)

            def chunk_scores(c_, a):
                pool.wait_ge(level_masked, a * BLK + (c_ + 1))
                steps.done(nc.gpsimd.tensor_tensor(masked[:, 0:4, :], masked[:, 0:4, :], masked[:, 4:8, :], ALU.add))
                steps.wait()
                steps.done(nc.gpsimd.tensor_tensor(masked[:, 0:2, :], masked[:, 0:2, :], masked[:, 2:4, :], ALU.add))
                steps.wait()
                if not isinstance(a, int) or a > 0:
                    pool.wait_ge(o_made, a)
                nc.gpsimd.tensor_tensor(scores[:, c_, :], masked[:, 0, :], masked[:, 1, :],
                                        ALU.add).then_inc(scores_done, 1)

            def decay_keys(h):
                pool.wait_ge(k_done, h + 1)
                pool.wait_ge(decays_done, h * 2 + 1)
                nc.gpsimd.tensor_tensor(qk[:, 0, :], qk[:, 0, :], k[:, :], ALU.mult).then_inc(keys_decayed, 1)
                pool.wait_ge(decays_done, h * 2 + 2)
                for n, half in enumerate(HALVES):
                    lv = qk[:, 2 + n, :].rearrange("p (b s h) -> p b s h", s=2, h=half)[:, :, 0, :]
                    kv = k[:, :].rearrange("p (b s h) -> p b s h", s=2, h=half)[:, :, 0, :]
                    nc.gpsimd.tensor_tensor(lv, lv, kv, ALU.mult).then_inc(keys_decayed, 1)

            def head(h, a):
                p = S["heads"] + 4 * h
                for j in range(4):
                    if h is not None:
                        low(p + j + 3, (j + 3) % RING)
                    if a is not None:
                        chunk_scores(j, a)
                if h is not None:
                    decay_keys(h)

            def head_steps(h, a):
                head(h, a)

            head(0, None)
            with steps.loop(1, HEADS_H, 2 * BLK) as h:
                head(h, h - 1)
            low(first + 32, first % RING)
            for j in range(BLK):
                chunk_scores(j, HEADS_H - 1)
            rest = first + 33
            n = (N_PANELS - rest) // RING
            with pool.Fori(0, n) as i:
                for j in range(RING):
                    low(i * RING + (rest + j), (rest + j) % RING)
            for p in range(rest + n * RING, N_PANELS):
                low(p, p % RING)

        @block.scalar
        def _(act):
            steps = Steps(act, act_steps)

            def high(p, p_int):
                if isinstance(p, int) and p >= N_PANELS:
                    return
                j = p_int % RING
                act.wait_ge(w_in[j], panel_loads(p, p_int))
                if not isinstance(p, int) or p >= RING:
                    act.wait_ge(made, p - RING + 1)
                nc.scalar.copy(w_hi[:, j, :], w_raw[:, j, :]).then_inc(w_high, 1)

            def panel_loads(p, p_int):
                if isinstance(p, int):
                    return 16 * (p // RING + 1)
                return p * 4 + (16 - 4 * (p_int % RING))

            def split(dst, src, scale=None):
                return nc.scalar.activation(dst, src, ACT.Copy, scale=1.0 if scale is None else scale)

            def root(r):
                act.wait_ge(var_ready, r + 1)
                nc.scalar.activation(var[:, :], var[:, :], ACT.Sqrt).then_inc(root_ready, 1)

            def square_x(s, m):
                if s > 0 or m >= 2:
                    act.wait_ge(summed, 8 * s + m - 1)
                nc.scalar.activation(squares[:, m % 2, :], x[:, m, :], ACT.Square).then_inc(squared, 1)

            def split_x(m, name):
                split(x_hi[:, m, :], x[:, m, :], gain(name, m)).then_inc(x_high, 1)

            act.wait_ge(c_in, 32)
            for m in range(DT):
                act.wait_ge(x_in, 16 * DT)
                square_x(S_MIX, m)
                split_x(m, "norm_mix")
                if m < 3:
                    high(m, m)
            for m in range(8):
                high(m + 3, m + 3)
                if m == 0:
                    root(R_MIX)
                t = zu[:, m, :] if m < 4 else zv[:, m - 4, :]
                act.wait_ge(evicted, m + 1)
                nc.scalar.activation(t, t, ACT.Gelu).then_inc(gelu_done, 1)
            for m in range(DT):
                high(S["ga"] + m + 3, S["ga"] + m + 3)
                if m < 4:
                    act.wait_ge(ln_var, m + 1)
                    nc.scalar.activation(ln_root[:, m:m + 1], ln_root[:, m:m + 1], ACT.Sqrt).then_inc(ln_rooted, 1)
                act.wait_ge(evicted, S["ga"] + m + 1)
                nc.scalar.activation(y[:, m, :], y[:, m, :], ACT.Sigmoid).then_inc(gate_a, 1)
            for gr in range(GROUPS):
                act.wait_ge(y_a, gr + 1)
                split(hid_hi[:, gr, :], zu[:, gr, :]).then_inc(hid_high, 1)
            for m in range(DT):
                high(S["upa"] + m + 3, S["upa"] + m + 3)

            def head(h, a):
                p = S["heads"] + 4 * h if h is not None else None

                if a is not None:
                    act.wait_ge(turned_v, a + 1)
                    nc.scalar.copy(v_nat[:, :, :], ps[:, 2, :].rearrange("p (b n) -> p b n", b=BLK)).then_inc(copied_v, 1)
                    act.wait_ge(turned_k, a + 1)
                    nc.scalar.copy(k_nat[:, :, :], ps[:, 3, 0:384].rearrange("p (b n) -> p b n", b=BLK - 1)).then_inc(copied_k, 1)
                if h is not None:
                    high(p + 3, S["heads"] + 3)
                    act.wait_ge(f_abs, h + 1)
                    steps.done(nc.scalar.activation(za[:, :], za[:, :], ACT.Exp, scale=-1.0))
                    steps.wait()
                    nc.scalar.activation(za[:, :], za[:, :], ACT.Ln, bias=1.0).then_inc(f_log, 1)
                    act.wait_ge(f_k, h + 1)
                    if a is not None:
                        act.wait_ge(diag_made, a + 1)
                        act.wait_ge(keys_decayed, a * (LEVELS + 1) + (LEVELS + 1))
                    nc.scalar.activation(k[:, :], za[:, :], ACT.Exp).then_inc(k_done, 1)
                    high(p + 4, S["heads"] + 4)
                    act.wait_ge(evicted, p + 2)
                    act.wait_ge(k_done, h + 1)
                    nc.scalar.activation(za[:, :], z[:, :], ACT.Exp, scale=-1.0).then_inc(q_exp, 1)
                    high(p + 5, S["heads"] + 5)
                    high(p + 6, S["heads"] + 6)
                if h is not None:
                    act.wait_ge(spans_done, h * 2 + 1)
                    nc.scalar.activation(qk[:, 0, :], qk[:, 0, :], ACT.Exp)
                    if a is not None:
                        act.wait_ge(o_made, a + 1)
                        act.wait_ge(states_done, a + 1)
                    nc.scalar.activation(qk[:, 1, :], cum[:, :], ACT.Exp)
                    nc.scalar.activation(chunk_decay[:, :], cum[:, P - 1:SEQ:P], ACT.Exp).then_inc(decays_done, 1)
                    act.wait_ge(spans_done, h * 2 + 2)
                    nc.scalar.activation(qk[:, 2:, :], qk[:, 2:, :], ACT.Exp).then_inc(decays_done, 1)
                if a is not None:
                    act.wait_ge(o_made, a + 1)
                    nc.scalar.activation(o_sq[:, :], ps[:, 7, :], ACT.Square).then_inc(o_squared, 1)
                    root(R_HEAD + a)
                    act.wait_ge(y_b, a + 1)
                    split(tile_at(hid_hi, a), o_tmp[:, :]).then_inc(hid_high, 1)
                if h is not None:
                    act.wait_ge(evicted, p + 4)
                    nc.scalar.activation(za[:, :], z[:, :], ACT.Exp, scale=-1.0).then_inc(o_exp, 1)

            head(0, None)
            with steps.loop(1, HEADS_H, 1) as h:
                head(h, h - 1)
            high(S["gb"] + 3, S["gb"] + 3)
            head(None, HEADS_H - 1)
            for m in range(DT):
                if m > 0:
                    high(S["gb"] + m + 3, S["gb"] + m + 3)
                act.wait_ge(evicted, S["gb"] + m + 1)
                nc.scalar.activation(gb[:, m, :], gb[:, m, :], ACT.Sigmoid).then_inc(gate_b, 1)
            for m in range(DT):
                high(S["upb"] + m + 3, S["upb"] + m + 3)
            for m in range(DT):
                act.wait_ge(y_mixed, m + 1)
                act.wait_ge(made, S["out1"])
                split(hid_hi[:, m, :], y[:, m, :]).then_inc(hid_high, 1)

            def residual(p0, s, name, feed=3):
                for m in range(DT):
                    high(p0 + m + feed, p0 + m + feed)
                    act.wait_ge(evicted, p0 + m + 1)
                    square_x(s, m)
                    if name:
                        split_x(m, name)

            residual(S["out1"], S_FFN, "norm_ffn")

            def ff1_up(ch, first):
                p0 = S["ff1"] + 16 * ch
                for m in range(DT):
                    high(p0 + m + 3, S["ff1"] + m + 3)
                    if first and m == 0:
                        root(R_FFN)
                    act.wait_ge(hid_raw, 8 * ch + (m + 1))
                    split(hid_hi[:, m, :], relu_sq[:, m % 2, :]).then_inc(hid_high, 1)

            def ff1_down(ch):
                for m in range(DT):
                    high(S["ff1"] + 16 * ch + (m + 11), S["ff1"] + m + 11)

            ff1_up(0, True)
            ff1_down(0)
            with act.Fori(1, FF1_CHUNKS - 1) as ch:
                ff1_up(ch, False)
                ff1_down(ch)
            ff1_up(FF1_CHUNKS - 1, False)
            residual(S["ff1"] + 16 * FF1_CHUNKS - 8, S_FINAL, None)

            root(R_FINAL)
            for m in range(DT):
                act.wait_ge(x_final, m + 1)
                square_x(S_ATTN0, m)
                split_x(m, "attn_0")

            for m in range(DT):
                high(S["conv_b"] + m + 3, S["conv_b"] + m + 3)
                if m == 0:
                    root(R_ATTN0)

            def conv_pair(m, m_int):
                p = S["conv_ch"] + 2 * m
                high(p + 3, S["conv_ch"] + 2 * m_int + 3)
                high(p + 4, S["conv_ch"] + 2 * m_int + 4)
                act.wait_ge(hid_raw, m + (8 * FF1_CHUNKS + 1))
                split(tile_at(hid_hi, m), conv_o[:, m_int % 2, :]).then_inc(hid_high, 1)

            with act.Fori(0, DT // 2) as i:
                for j in range(2):
                    conv_pair(i * 2 + j, j)
            residual(S["out2"], S_FFN0, "ffn_0")

            def ffn(l):
                base = S[f"ffn_{l}"]
                raw0 = 8 * FF1_CHUNKS + DT + l * FF2_TILES
                p0, t0 = base, 0
                for n, size in enumerate(FF2_CHUNKS):
                    def pair(m, m_int, first):
                        p = p0 + 2 * m
                        high(p + 3, p0 + 2 * m_int + 3)
                        if first:
                            root(R_FFN1 if l else R_FFN0)
                        act.wait_ge(conv_done, m + (l * FF2_TILES + t0 + 1))
                        nc.scalar.activation(conv_u[:, m_int % 2, :], conv_u[:, m_int % 2, :],
                                             ACT.Silu).then_inc(silu_done, 1)
                        high(p + 4, p0 + 2 * m_int + 4)
                        act.wait_ge(hid_raw, m + (raw0 + t0 + 1))
                        split(tile_at(hid_hi, m), conv_o[:, m_int % 2, :]).then_inc(hid_high, 1)

                    pair(0, 0, n == 0)
                    pair(1, 1, False)
                    with act.Fori(1, size // 2) as i:
                        for j in range(2):
                            pair(i * 2 + j, j, False)
                    p0 += 2 * size
                    t0 += size
                    if n == len(FF2_CHUNKS) - 1 and l == 0:
                        residual(p0, S_ATTN1, "kv")
                    else:
                        for m in range(DT):
                            high(p0 + m + 3, p0 + m + 3)
                    p0 += DT

            ffn(0)

            for m in range(DT):
                high(S["k"] + m + 3, S["k"] + m + 3)
                if m == 0:
                    root(R_ATTN1)
                act.wait_ge(evicted, S["k"] + m + 1)
                nc.scalar.activation(k_sq[:, m % 2, :], k_raw[:, m % 2, :], ACT.Square).then_inc(k_squared, 1)
                if m > 0:
                    root(R_K + m - 1)
            for m in range(DT):
                high(S["v"] + m + 3, S["v"] + m + 3)
                if m == 0:
                    root(R_K + DT - 1)
                act.wait_ge(v_spread, m + 1)
                nc.scalar.copy(v_all[:, m, :], ps[:, 2 + m % 2, :]).then_inc(v_copied, 1)
            high(S["f"] + 3, S["f"] + 3)
            for m in range(DT):
                act.wait_ge(made, S["qg"])
                split_x(m, "attn_1")
            rows16 = slice(0, HEADS_A)
            act.wait_ge(l_abs, 1)
            steps.done(nc.scalar.activation(logit_a[rows16, :], logit_a[rows16, :], ACT.Exp, scale=-1.0))
            steps.wait()
            nc.scalar.activation(logit_a[rows16, :], logit_a[rows16, :], ACT.Ln, bias=1.0).then_inc(l_log, 1)

            def copy_bias(t):
                act.wait_ge(biased, t + 1)
                nc.scalar.copy(key_bias[:, :], ps[:, 7, :]).then_inc(bias_read, 1)

            def softmax(t):
                for b in range(BLK):
                    act.wait_ge(maxed, t * BLK + (b + 1))
                    at = prob[:, OFF_P[b]:OFF_P[b] + P * (b + 1)]
                    ins = nc.scalar.activation(at, at, ACT.Exp, bias=row_neg[:, b:b + 1],
                                               accum_out=row_sum[:, b:b + 1])
                ins.then_inc(exped, 1)

            def copy_prob(t, t_int):
                for b in (0, 2):
                    act.wait_ge(turned_p, t * BLK + (b + 1))
                    nc.scalar.copy(prob_t[:, OFF_T[b]:OFF_T[b] + SEQ - P * b],
                                   ps[:, 5 + b % 2, P * b:SEQ]).then_inc(copied_even, 1)

            def pair(m, m_int, a):
                p = S["qg"] + 2 * m if m is not None else None
                if a is not None:
                    if not isinstance(a, int) or a > 0:
                        act.wait_ge(attended, 2 * a)
                    nc.scalar.copy(k_now[:, :], tile_at(k_all, a)).then_inc(head_loaded, 1)
                    nc.scalar.copy(v_now[:, :], tile_at(v_all, a)).then_inc(head_loaded, 1)
                    copy_bias(2 * a)
                    softmax(2 * a)
                if m is not None:
                    high(p + 3, S["qg"] + 2 * m_int + 3)
                    act.wait_ge(evicted, p + 1)
                    nc.scalar.activation(q_sq[:, :], q_raw[:, :], ACT.Square).then_inc(q_squared, 1)
                if a is not None:
                    copy_prob(2 * a, 0)
                    copy_bias(2 * a + 1)
                    softmax(2 * a + 1)
                if m is not None:
                    high(p + 4, S["qg"] + 2 * m_int + 4)
                    act.wait_ge(evicted, p + 2)
                    nc.scalar.activation(gate[:, m_int % 2, :], gate[:, m_int % 2, :], ACT.Exp,
                                         scale=-1.0).then_inc(gate_g, 1)
                if a is not None:
                    copy_prob(2 * a + 1, 1)
                if m is not None:
                    root(R_Q + m)
                if a is not None:
                    act.wait_ge(attn_read, 2 * a + 2)
                    split(tile_at(hid_hi, a), o_all[:, :]).then_inc(hid_high, 1)

            pair(0, 0, None)
            with act.Fori(0, DT // 2 - 1) as i:
                pair(i * 2 + 1, 1, i * 2)
                pair(i * 2 + 2, 2, i * 2 + 1)
            pair(DT - 1, DT - 1, DT - 2)
            high(S["out3"] + 3, S["out3"] + 3)
            pair(None, None, DT - 1)
            for m in range(DT):
                if m > 0:
                    high(S["out3"] + m + 3, S["out3"] + m + 3)
                act.wait_ge(evicted, S["out3"] + m + 1)
                square_x(S_FFN1, m)
                split_x(m, "ffn_1")
            ffn(1)

        @block.vector
        def _(dve):
            v = nc.vector
            steps = Steps(dve, dve_steps)

            def link(ins):
                steps.done(ins)
                steps.wait()

            def bank(p_int):
                return ps[:, p_int % 2, :]

            def wait_made(p):
                dve.wait_ge(made, p + 1)

            def scale_out(dst, p, p_int):
                wait_made(p)
                return v.tensor_tensor(dst, bank(p_int), inv_rms[:, :], ALU.mult)

            def norm(r, inv_n, bank_n, dst):
                dve.wait_ge(sums_ready, r + 1)
                v.tensor_scalar(var[:, :], ps[:, bank_n, :], inv_n, EPS, ALU.mult, ALU.add).then_inc(var_ready, 1)
                dve.wait_ge(root_ready, r + 1)
                return v.reciprocal(dst, var[:, :])

            def sum_squares(s, m):
                dve.wait_ge(squared, 8 * s + m + 1)
                if m == 0:
                    if s > 0:
                        pass
                    v.tensor_copy(sum_sq[:, :], squares[:, 0, :]).then_inc(summed, 1)
                else:
                    dve.wait_ge(summed, 8 * s + m)
                    v.tensor_tensor(sum_sq[:, :], sum_sq[:, :], squares[:, m % 2, :], ALU.add).then_inc(summed, 1)

            def low_x(n, m, name):
                dve.wait_ge(x_high, 8 * n + m + 1)
                v.scalar_tensor_tensor(x_lo[:, m, :], x[:, m, :], gain(name, m), x_hi[:, m, :].bitcast(F),
                                       ALU.mult, ALU.subtract).then_inc(x_low, 1)

            def low_hid(count, m, src):
                dve.wait_ge(hid_high, count)
                v.tensor_tensor(tile_at(hid_lo, m), src, tile_at(hid_hi, m).bitcast(F),
                                ALU.subtract).then_inc(hid_low, 1)

            def residual(p0, s, n, name):
                for m in range(DT):
                    wait_made(p0 + m)
                    v.tensor_tensor(x[:, m, :], x[:, m, :], bank(p0 + m), ALU.add).then_inc(evicted, 1)
                    if s is not None:
                        sum_squares(s, m)
                    if name:
                        low_x(n, m, name)

            dve.wait_ge(c_in, 32)
            v.tensor_copy(identb[:, :], c("ident")).then_inc(consts_ok, 1)
            v.tensor_copy(negb[:, :], c("neg")).then_inc(consts_ok, 1)
            for m in range(DT):
                sum_squares(S_MIX, m)
                low_x(X_MIX, m, "norm_mix")
            dve.wait_ge(row_in, 32)
            v.memset(ws_sb[P // 2:P, :, 0:P // 2], 0.0).then_inc(ws_masked, 1)
            link(norm(R_MIX, 1.0 / D, 7, inv_rms[:, :]))
            for m in range(8):
                scale_out(zu[:, m, :] if m < 4 else zv[:, m - 4, :], m, m).then_inc(evicted, 1)
            lng, lnb, bs = rows_sb[:, 0, :], rows_sb[:, 1, :], rows_sb[:, 2, :]

            def layer_norm(b):
                dve.wait_ge(v_turned, b + 1)
                src = ps[:, 2 + b % 2, :]
                link(v.bn_stats(ln_stats[:, b, :], src))
                link(v.bn_aggr(ln_mv[:, b, :], ln_stats[:, b, :]))
                v.tensor_scalar(ln_root[:, b:b + 1], ln_mv[:, b, 1:2], EPS, None, ALU.add).then_inc(ln_var, 1)
                dve.wait_ge(ln_rooted, b + 1)
                link(v.reciprocal(ln_inv[:, b:b + 1], ln_root[:, b:b + 1]))
                link(v.tensor_scalar(vn[:, b, :], src, ln_mv[:, b, 0:1], ln_inv[:, b:b + 1],
                                     ALU.subtract, ALU.mult))
                link(v.tensor_tensor(vn[:, b, :], vn[:, b, :], lng, ALU.mult))
                v.tensor_tensor(vn[:, b, :], vn[:, b, :], lnb, ALU.add).then_inc(v_normed, 1)

            for m in range(DT):
                if m < 4:
                    layer_norm(m)
                scale_out(y[:, m, :], S["ga"] + m, m).then_inc(evicted, 1)
            for gr in range(GROUPS):
                dve.wait_ge(mixed, gr + 1)
                bias = bs[:, gr * P:(gr + 1) * P].unsqueeze(1).broadcast_to([P, BLK, P])
                v.tensor_tensor(zv[:, gr, :].rearrange("p (b n) -> p b n", b=BLK),
                                ps[:, 2 + gr % 2, :].rearrange("p (b n) -> p b n", b=BLK),
                                bias, ALU.add).then_inc(mixed_read, 1)
                dve.wait_ge(mixed_read, gr + 1)
                v.tensor_tensor(zu[:, gr, :], zu[:, gr, :], zv[:, gr, :], ALU.mult).then_inc(y_a, 1)
                low_hid(HID_GMLP + gr + 1, gr, zu[:, gr, :])
            for m in range(DT):
                wait_made(S["upa"] + m)
                dve.wait_ge(gate_a, m + 1)
                v.tensor_tensor(y[:, m, :], y[:, m, :], bank(S["upa"] + m), ALU.mult).then_inc(evicted, 1)

            def mask_chunk(c_, a):
                dve.wait_ge(level_made, a * BLK + (c_ + 1))
                if c_ > 0 or not isinstance(a, int) or a > 0:
                    dve.wait_ge(scores_done, a * BLK + c_)
                lv = c("levels").rearrange("p (l n) -> p l n", l=LEVELS)
                v.tensor_tensor(masked[:, 0:4, :], ps[:, 4, :].rearrange("p (l n) -> p l n", l=4),
                                lv[:, 0:4, :], ALU.mult)
                v.tensor_tensor(masked[:, 4:LEVELS, :], ps[:, 5, 0:(LEVELS - 4) * P].rearrange("p (l n) -> p l n", n=P),
                                lv[:, 4:LEVELS, :], ALU.mult)
                v.tensor_tensor(masked[:, LEVELS, :], ps[:, 6, c_ * P:(c_ + 1) * P], c("ident"),
                                ALU.mult).then_inc(level_masked, 1)

            def states(a):
                dve.wait_ge(kv_made, a + 1)
                link(v.tensor_copy(state[:, 0, :], ps[:, 3, 0:P]))
                for n in range(1, BLK - 1):
                    ins = v.scalar_tensor_tensor(state[:, n, :], state[:, n - 1, :], chunk_decay[:, n:n + 1],
                                                 ps[:, 3, n * P:(n + 1) * P], ALU.mult, ALU.add)
                    if n < BLK - 2:
                        link(ins)
                ins.then_inc(states_done, 1)

            def spans(h):
                last = cum[:, P - 1:SEQ:P].unsqueeze(2).broadcast_to([P, BLK, P])
                v.tensor_tensor(qk[:, 0, :].rearrange("p (b n) -> p b n", b=BLK), last,
                                cum[:, :].rearrange("p (b n) -> p b n", b=BLK), ALU.subtract).then_inc(spans_done, 1)
                for n, half in enumerate(HALVES):
                    lv = qk[:, 2 + n, :].rearrange("p (b s h) -> p b s h", s=2, h=half)
                    cu = cum[:, :].rearrange("p (b s h) -> p b s h", s=2, h=half)
                    mid = cu[:, :, 0, half - 1:half].broadcast_to([P, SEQ // (2 * half), half])
                    v.tensor_tensor(lv[:, :, 0, :], mid, cu[:, :, 0, :], ALU.subtract)
                    ins = v.tensor_tensor(lv[:, :, 1, :], cu[:, :, 1, :], mid, ALU.subtract)
                ins.then_inc(spans_done, 1)

            def decay_queries(h):
                dve.wait_ge(decays_done, h * 2 + 1)
                v.tensor_tensor(qk[:, 1, :], qk[:, 1, :], q[:, :], ALU.mult).then_inc(queries_decayed, 1)
                dve.wait_ge(decays_done, h * 2 + 2)
                for n, half in enumerate(HALVES):
                    lv = qk[:, 2 + n, :].rearrange("p (b s h) -> p b s h", s=2, h=half)[:, :, 1, :]
                    qv = q[:, :].rearrange("p (b s h) -> p b s h", s=2, h=half)[:, :, 1, :]
                    v.tensor_tensor(lv, lv, qv, ALU.mult).then_inc(queries_decayed, 1)

            def swish(dst, exped_sem, h):
                dve.wait_ge(exped_sem, h + 1)
                link(v.tensor_scalar(za[:, :], za[:, :], 1.0, None, ALU.add))
                link(v.reciprocal(za[:, :], za[:, :]))
                return v.tensor_tensor(dst, z[:, :], za[:, :], ALU.mult)

            def head(h, a):
                p, p4 = (S["heads"] + 4 * h, S["heads"]) if h is not None else (None, None)
                if h is not None:
                    if a is not None:
                        dve.wait_ge(o_gate, h)
                    scale_out(z[:, :], p, p4).then_inc(evicted, 1)
                    dve.wait_ge(evicted, p + 1)
                    v.scalar_tensor_tensor(za[:, :], z[:, :], -1.0, z[:, :], ALU.mult, ALU.max).then_inc(f_abs, 1)
                    dve.wait_ge(f_log, h + 1)
                    link(v.scalar_tensor_tensor(g[:, :], z[:, :], 0.0, za[:, :], ALU.min, ALU.subtract))
                    v.tensor_tensor(za[:, :], g[:, :], z[:, :], ALU.subtract).then_inc(f_k, 1)
                    v.tensor_tensor_scan(cum[:, :], c("reset"), g[:, :], 0.0, ALU.mult, ALU.add).then_inc(cum_done, 1)
                if a is not None:
                    mask_chunk(0, a)
                if h is not None:
                    dve.wait_ge(cum_done, h + 1)
                    scale_out(z[:, :], p + 1, p4 + 1).then_inc(evicted, 1)
                    if a is not None:
                        dve.wait_ge(diag_made, a + 1)
                    swish(q[:, :], q_exp, h).then_inc(q_done, 1)
                if a is not None:
                    mask_chunk(1, a)
                    states(a)
                if h is not None:
                    if a is not None:
                        dve.wait_ge(turned_v, a + 1)
                    scale_out(vT[:, :], p + 2, p4 + 2).then_inc(evicted, 1)
                if a is not None:
                    mask_chunk(2, a)
                    mask_chunk(3, a)
                if h is not None:
                    dve.wait_ge(cum_done, h + 1)
                    spans(h)
                    dve.wait_ge(q_done, h + 1)
                    decay_queries(h)
                if a is not None:
                    link(norm(R_HEAD + a, 1.0 / P, 2, o_inv[:, :]))
                    link(v.scalar_tensor_tensor(o_tmp[:, :], ps[:, 7, :], gain("hg_norm"), o_inv[:, :],
                                                ALU.mult, ALU.mult))
                    dve.wait_ge(o_gate, a + 1)
                    v.tensor_tensor(o_tmp[:, :], o_tmp[:, :], silu_o[:, :], ALU.mult).then_inc(y_b, 1)
                    low_hid(a + (HID_HEADS + 1), a, o_tmp[:, :])
                if h is not None:
                    scale_out(z[:, :], p + 3, p4 + 3).then_inc(evicted, 1)
                    swish(silu_o[:, :], o_exp, h).then_inc(o_gate, 1)

            head(0, None)
            with steps.loop(1, HEADS_H, 9) as h:
                head(h, h - 1)
            head(None, HEADS_H - 1)
            for m in range(DT):
                scale_out(gb[:, m, :], S["gb"] + m, m).then_inc(evicted, 1)
            for m in range(DT):
                wait_made(S["upb"] + m)
                dve.wait_ge(gate_b, m + 1)
                v.tensor_tensor(gy[:, m % 2, :], gb[:, m, :], bank(m), ALU.mult).then_inc(evicted, 1)
                dve.wait_ge(evicted, S["upb"] + m + 1)
                v.tensor_tensor(y[:, m, :], y[:, m, :], gy[:, m % 2, :], ALU.add).then_inc(y_mixed, 1)
            for m in range(DT):
                low_hid(HID_MIX + m + 1, m, y[:, m, :])
            residual(S["out1"], S_FFN, X_FFN, "norm_ffn")

            def ff1_up(ch, first):
                p0 = S["ff1"] + 16 * ch
                for m in range(DT):
                    if first and m == 0:
                        link(norm(R_FFN, 1.0 / D, 7, inv_rms[:, :]))
                    scale_out(relu[:, m % 2, :], p0 + m, m).then_inc(evicted, 1)
                    dve.wait_ge(evicted, p0 + (m + 1))
                    v.scalar_tensor_tensor(relu_sq[:, m % 2, :], relu[:, m % 2, :], 0.0, relu[:, m % 2, :],
                                           ALU.max, ALU.mult).then_inc(hid_raw, 1)
                    low_hid(8 * ch + (HID_FF1 + m + 1), m, relu_sq[:, m % 2, :])

            def ff1_down(ch):
                for m in range(DT):
                    wait_made(S["ff1"] + 16 * ch + (8 + m))
                    v.tensor_tensor(x[:, m, :], x[:, m, :], bank(m), ALU.add).then_inc(evicted, 1)

            ff1_up(0, True)
            ff1_down(0)
            with dve.Fori(1, FF1_CHUNKS - 1) as ch:
                ff1_up(ch, False)
                ff1_down(ch)
            ff1_up(FF1_CHUNKS - 1, False)
            residual(S["ff1"] + 16 * FF1_CHUNKS - 8, S_FINAL, None, None)
            link(norm(R_FINAL, 1.0 / D, 7, inv_rms[:, :]))
            for m in range(DT):
                v.scalar_tensor_tensor(x[:, m, :], x[:, m, :], gain("final_norm", m), inv_rms[:, :],
                                       ALU.mult, ALU.mult).then_inc(x_final, 1)
                sum_squares(S_ATTN0, m)
                low_x(X_ATTN0, m, "attn_0")

            v.memset(padded[:, :, 0:2], 0.0)
            link(norm(R_ATTN0, 1.0 / D, 7, inv_rms[:, :]))
            for m in range(DT):
                scale_out(conv_b[:, m, :], S["conv_b"] + m, S["conv_b"] + m).then_inc(evicted, 1)

            def convolve(dst, src, taps):
                link(v.tensor_scalar(dst, src[:, 2:SEQ + 2], taps[2], None, ALU.mult))
                link(v.scalar_tensor_tensor(dst, src[:, 1:SEQ + 1], taps[1], dst, ALU.mult, ALU.add))
                return v.scalar_tensor_tensor(dst, src[:, 0:SEQ], taps[0], dst, ALU.mult, ALU.add)

            def conv_pair(m, j):
                p = S["conv_ch"] + 2 * m
                scale_out(conv_c[:, j, :], p, S["conv_ch"]).then_inc(evicted, 1)
                scale_out(conv_t[:, j, :], p + 1, S["conv_ch"] + 1).then_inc(evicted, 1)
                dve.wait_ge(evicted, p + 2)
                link(v.tensor_tensor(padded[:, j, 2:SEQ + 2], conv_c[:, j, :], conv_t[:, j, :], ALU.mult))
                link(convolve(conv_u[:, j, :], padded[:, j, :], [gain("a_conv", m + t * DT) for t in range(3)]))
                v.tensor_tensor(conv_o[:, j, :], conv_u[:, j, :], tile_at(conv_b, m),
                                ALU.mult).then_inc(hid_raw, 1)
                low_hid(m + (HID_CONV + 1), m, conv_o[:, j, :])

            with steps.loop(0, DT // 2, 8) as i:
                for j in range(2):
                    conv_pair(i * 2 + j, j)
            residual(S["out2"], S_FFN0, X_FFN0, "ffn_0")

            def ffn(l):
                p0, t0 = S[f"ffn_{l}"], 0
                hid0 = HID_FFN1 if l else HID_FFN0
                v.memset(padded[:, :, 0:2], 0.0)
                link(norm(R_FFN1 if l else R_FFN0, 1.0 / D, 7, inv_rms[:, :]))
                for n, size in enumerate(FF2_CHUNKS):
                    def pair(m, j):
                        p = p0 + 2 * m
                        scale_out(padded[:, j, 2:SEQ + 2], p, p0).then_inc(evicted, 1)
                        dve.wait_ge(evicted, p + 1)
                        convolve(conv_u[:, j, :], padded[:, j, :],
                                 [gain(f"conv_{l}", m + (t * FF2_TILES + t0)) for t in range(3)]).then_inc(conv_done, 1)
                        scale_out(conv_t[:, j, :], p + 1, p0 + 1).then_inc(evicted, 1)
                        dve.wait_ge(evicted, p + 2)
                        dve.wait_ge(silu_done, m + (l * FF2_TILES + t0 + 1))
                        v.tensor_tensor(conv_o[:, j, :], conv_u[:, j, :], conv_t[:, j, :],
                                        ALU.mult).then_inc(hid_raw, 1)
                        low_hid(m + (hid0 + t0 + 1), m, conv_o[:, j, :])

                    pair(0, 0)
                    pair(1, 1)
                    with steps.loop(1, size // 2, 4) as i:
                        for j in range(2):
                            pair(i * 2 + j, j)
                    p0 += 2 * size
                    t0 += size
                    last = n == len(FF2_CHUNKS) - 1
                    if last and l == 0:
                        residual(p0, S_ATTN1, X_KV, "kv")
                    else:
                        for m in range(DT):
                            wait_made(p0 + m)
                            v.tensor_tensor(x[:, m, :], x[:, m, :], bank(p0 + m), ALU.add).then_inc(evicted, 1)
                    p0 += DT

            ffn(0)

            link(norm(R_ATTN1, 1.0 / D, 7, inv_rms[:, :]))

            def norm_k(m):
                link(norm(R_K + m, 1.0 / HEAD_DIM, 7, k_inv[:, :]))
                v.scalar_tensor_tensor(k_all[:, m, :], k_raw[:, m % 2, :], gain("k_norm"), k_inv[:, :],
                                       ALU.mult, ALU.mult).then_inc(k_normed, 1)

            for m in range(DT):
                if m >= 2:
                    dve.wait_ge(k_normed, m - 1)
                scale_out(k_raw[:, m % 2, :], S["k"] + m, S["k"] + m).then_inc(evicted, 1)
                if m > 0:
                    norm_k(m - 1)
            for m in range(DT):
                if m >= 2:
                    dve.wait_ge(v_spread, m - 1)
                scale_out(v_raw[:, m % 2, :], S["v"] + m, S["v"] + m).then_inc(evicted, 1)
                if m == 0:
                    norm_k(DT - 1)
            r16 = slice(0, HEADS_A)
            p = S["f"]
            wait_made(p)
            dve.wait_ge(v_spread, DT)
            dve.wait_ge(v_copied, DT)
            v.tensor_tensor(logit[r16, :], ps[r16, p % 2, :], inv_rms[r16, :], ALU.mult).then_inc(evicted, 1)
            dve.wait_ge(evicted, p + 1)
            b_at = PARAM_COLS["b_f"][0]
            link(v.tensor_scalar(logit[r16, :], logit[r16, :], params[r16, b_at:b_at + 1], None, ALU.add))
            v.scalar_tensor_tensor(logit_a[r16, :], logit[r16, :], -1.0, logit[r16, :], ALU.mult,
                                   ALU.max).then_inc(l_abs, 1)
            for m in range(DT):
                low_x(X_Q, m, "attn_1")
            dve.wait_ge(l_log, 1)
            link(v.scalar_tensor_tensor(logit[r16, :], logit[r16, :], 0.0, logit_a[r16, :], ALU.min, ALU.subtract))
            a1, _ = CONST_COLS["ones"]
            link(v.tensor_tensor_scan(log_c[r16, :], consts[r16, a1:a1 + 1].broadcast_to([HEADS_A, SEQ]), logit[r16, :], 0.0,
                                      ALU.mult, ALU.add))

            def pick(t):
                if not isinstance(t, int) or t > 0:
                    dve.wait_ge(biased, t)
                hot = CONST_COLS["onehot"][0]
                v.tensor_scalar(log_pick[r16, :], log_c[r16, :], column(consts, hot + t, HEADS_A), None,
                                ALU.mult).then_inc(picked, 1)

            SC = [(3, 384), (4, 0), (3, 0), (2, 0)]

            def maxima(t):
                dve.wait_ge(bias_read, t + 1)
                dve.wait_ge(scored, t + 1)
                if not isinstance(t, int) or t > 0:
                    dve.wait_ge(turned_p, t * BLK)
                v.memset(wait_mark[:, :], 0.0)
                for b in range(BLK):
                    n = P * (b + 1)
                    bk, at = SC[b]
                    link(v.tensor_tensor_reduce(out=prob[:, OFF_P[b]:OFF_P[b] + n], in0=ps[:, bk, at:at + n],
                                                in1=key_bias[:, 0:n], scale=1.0, scalar=-3e38,
                                                op0=ALU.add, op1=ALU.max, accum_out=row_max[:, b:b + 1]))
                    v.tensor_scalar(row_neg[:, b:b + 1], row_max[:, b:b + 1], -1.0, None,
                                    ALU.mult).then_inc(maxed, 1)

            def scale_prob(t):
                dve.wait_ge(exped, t + 1)
                link(v.reciprocal(row_inv[:, :], row_sum[:, :]))
                for b in range(BLK):
                    at = prob[:, OFF_P[b]:OFF_P[b] + P * (b + 1)]
                    v.tensor_scalar(at, at, row_inv[:, b:b + 1], None, ALU.mult).then_inc(scaled, 1)

            def copy_prob(t):
                for b in (1, 3):
                    dve.wait_ge(turned_p, t * BLK + (b + 1))
                    v.tensor_copy(prob_t[:, OFF_T[b]:OFF_T[b] + SEQ - P * b],
                                  ps[:, 5 + b % 2, P * b:SEQ]).then_inc(copied_odd, 1)

            def take_output(t, side, par):
                rows_ = slice(side * HEAD_DIM, (side + 1) * HEAD_DIM)
                dve.wait_ge(attended, t + 1)
                bk = 7 if side == 0 else 2
                return v.tensor_tensor(o_all[rows_, :], ps[rows_, bk, :], gate[rows_, par, :], ALU.mult)

            def pair(m, par, a):
                p = S["qg"] + 2 * m if m is not None else None
                if a is not None:
                    pick(2 * a)
                    maxima(2 * a)
                    scale_prob(2 * a)
                if m is not None:
                    scale_out(q_raw[:, :], p, S["qg"]).then_inc(evicted, 1)
                if a is not None:
                    pick(2 * a + 1)
                    copy_prob(2 * a)
                    maxima(2 * a + 1)
                    scale_prob(2 * a + 1)
                if m is not None:
                    scale_out(gate[:, par, :], p + 1, S["qg"] + 1).then_inc(evicted, 1)
                if a is not None:
                    take_output(2 * a, 0, 1 - par if m is not None else 1).then_inc(attn_read, 1)
                    copy_prob(2 * a + 1)
                if m is not None:
                    dve.wait_ge(gate_g, m + 1)
                    link(v.tensor_scalar(gate[:, par, :], gate[:, par, :], 1.0, None, ALU.add))
                    link(v.reciprocal(gate[:, par, :], gate[:, par, :]))
                    link(norm(R_Q + m, 1.0 / HEAD_DIM, 3, q_inv[:, :]))
                    link(v.scalar_tensor_tensor(q_n[:, :], q_raw[:, :], gain("q_norm"), q_inv[:, :],
                                                ALU.mult, ALU.mult))
                    v.tensor_scalar(q_n[:, :], q_n[:, :], HEAD_DIM ** -0.5, None, ALU.mult).then_inc(q_normed, 1)
                if a is not None:
                    take_output(2 * a + 1, 1, 1 - par if m is not None else 1).then_inc(attn_read, 1)
                    low_hid(a + (HID_ATTN + 1), a, o_all[:, :])

            pair(0, 0, None)
            with steps.loop(0, DT // 2 - 1, 2 * 14) as i:
                pair(i * 2 + 1, 1, i * 2)
                pair(i * 2 + 2, 0, i * 2 + 1)
            pair(DT - 1, 1, DT - 2)
            pair(None, None, DT - 1)
            residual(S["out3"], S_FFN1, X_FFN1, "ffn_1")
            ffn(1)

        @block.tensor
        def _(pe):
            def product(p, p_int, hi, lo, tiles=DT, ready=None, done=None, rows_=None):
                j = p_int % RING
                pe.wait_ge(w_low, p + 1)
                if not isinstance(p, int) or p >= 2:
                    pe.wait_ge(evicted, p - 1)
                for kt in range(tiles):
                    if ready is not None:
                        pe.wait_ge(ready, done + (kt + 1))
                    wh, wl = w_hi[:, j, kt * P:(kt + 1) * P], w_lo[:, j, kt * P:(kt + 1) * P]
                    o = ps[:, p_int % 2, :]
                    nc.tensor.matmul(o, wh, hi[:, kt, :], start=(kt == 0), stop=False)
                    nc.tensor.matmul(o, wh, lo[:, kt, :], start=False, stop=False)
                    ins = nc.tensor.matmul(o, wl, hi[:, kt, :], start=False, stop=(kt == tiles - 1))
                ins.then_inc(made, 1)

            def sums(bank_n, weights, src):
                nc.tensor.matmul(ps[:, bank_n, :], weights, src, start=True, stop=True).then_inc(sums_ready, 1)

            def stream_sums(s):
                pe.wait_ge(summed, 8 * s + 8)
                sums(7, c("ones"), sum_sq[:, :])

            def linear(p0, n, hi, lo, ready, done, tiles=DT, stream=None):
                for m in range(n):
                    product(p0 + m, p0 + m, hi, lo, tiles, ready if m == 0 else None, done)
                    if m == 0 and stream is not None:
                        stream_sums(stream)

            pe.wait_ge(consts_ok, 2)
            linear(S["zu"], 8, x_hi, x_lo, x_low, 8 * X_MIX, stream=S_MIX)

            def turn_zv(b):
                if b >= 2:
                    pe.wait_ge(v_normed, b - 1)
                for gr in range(GROUPS):
                    pe.wait_ge(gelu_done, 4 + gr + 1)
                    ins = nc.tensor.transpose(ps[:, 2 + b % 2, gr * P:(gr + 1) * P],
                                              zv[:, gr, b * P:(b + 1) * P], c("ident"))
                ins.then_inc(v_turned, 1)

            for m in range(DT):
                product(S["ga"] + m, S["ga"] + m, x_hi, x_lo)
                if 1 <= m < 5:
                    turn_zv(m - 1)
            pe.wait_ge(ws_masked, 1)
            for gr in range(GROUPS):
                pe.wait_ge(v_normed, BLK)
                if gr >= 2:
                    pe.wait_ge(mixed_read, gr - 1)
                for b in range(BLK):
                    ins = nc.tensor.matmul(ps[:, 2 + gr % 2, b * P:(b + 1) * P], vn[:, b, gr * P:(gr + 1) * P],
                                           ws_sb[:, gr, :], start=True, stop=True)
                ins.then_inc(mixed, 1)
            linear(S["upa"], DT, hid_hi, hid_lo, hid_low, HID_GMLP, tiles=GROUPS)

            def turns(a):
                pe.wait_ge(evicted, a * 4 + (S["heads"] + 3))
                if not isinstance(a, int) or a > 0:
                    pe.wait_ge(var_ready, a + (R_HEAD))
                for b in range(BLK):
                    ins = nc.tensor.transpose(ps[:, 2, b * P:(b + 1) * P], vT[:, b * P:(b + 1) * P], c("ident"))
                ins.then_inc(turned_v, 1)
                pe.wait_ge(keys_decayed, a * (LEVELS + 1) + 1)
                if not isinstance(a, int) or a > 0:
                    pe.wait_ge(states_done, a)
                for b in range(BLK - 1):
                    ins = nc.tensor.transpose(ps[:, 3, b * P:(b + 1) * P], qk[:, 0, b * P:(b + 1) * P], c("ident"))
                ins.then_inc(turned_k, 1)
                pe.wait_ge(q_done, a + 1)
                pe.wait_ge(k_done, a + 1)
                if not isinstance(a, int) or a > 0:
                    pe.wait_ge(level_masked, a * BLK)
                for b in range(BLK):
                    at = slice(b * P, (b + 1) * P)
                    ins = nc.tensor.matmul(ps[:, 6, at], k[:, at], q[:, at], start=True, stop=True)
                ins.then_inc(diag_made, 1)

            def levels(c_, a):
                if c_ == 0:
                    pe.wait_ge(keys_decayed, a * (LEVELS + 1) + (LEVELS + 1))
                    pe.wait_ge(queries_decayed, a * (LEVELS + 1) + (LEVELS + 1))
                if c_ > 0 or not isinstance(a, int) or a > 0:
                    pe.wait_ge(level_masked, a * BLK + c_)
                at = slice(c_ * P, (c_ + 1) * P)
                for n in range(LEVELS):
                    ins = nc.tensor.matmul(ps[:, 4 + n // 4, (n % 4) * P:(n % 4 + 1) * P], qk[:, 2 + n, at],
                                           qk[:, 2 + n, at], start=True, stop=True)
                ins.then_inc(level_made, 1)

            def chunk_kv(a):
                pe.wait_ge(copied_v, a + 1)
                pe.wait_ge(copied_k, a + 1)
                for b in range(BLK - 1):
                    ins = nc.tensor.matmul(ps[:, 3, b * P:(b + 1) * P], k_nat[:, b, :], v_nat[:, b, :],
                                           start=True, stop=True)
                ins.then_inc(kv_made, 1)

            def outputs(a):
                if not isinstance(a, int) or a > 0:
                    pe.wait_ge(y_b, a)
                pe.wait_ge(states_done, a + 1)
                for b in range(BLK):
                    at = slice(b * P, (b + 1) * P)
                    pe.wait_ge(scores_done, a * BLK + (b + 1))
                    ins = nc.tensor.matmul(ps[:, 7, at], v_nat[:, b, :], scores[:, b, :], start=True, stop=(b == 0))
                    if b > 0:
                        ins = nc.tensor.matmul(ps[:, 7, at], state[:, b - 1, :], qk[:, 1, at], start=False, stop=True)
                ins.then_inc(o_made, 1)

            def output_sums(a):
                pe.wait_ge(o_squared, a + 1)
                sums(2, c("ones"), o_sq[:, :])

            def head(h, a):
                p, p4 = (S["heads"] + 4 * h, S["heads"]) if h is not None else (S["gb"], S["gb"])
                if a is not None:
                    turns(a)
                product(p, p4, x_hi, x_lo)
                if a is not None:
                    levels(0, a)
                product(p + 1, p4 + 1, x_hi, x_lo)
                if a is not None:
                    levels(1, a)
                    chunk_kv(a)
                product(p + 2, p4 + 2, x_hi, x_lo)
                if a is not None:
                    levels(2, a)
                    levels(3, a)
                    outputs(a)
                product(p + 3, p4 + 3, x_hi, x_lo)
                if a is not None:
                    output_sums(a)

            head(0, None)
            with pe.Fori(1, HEADS_H) as h:
                head(h, h - 1)
            a = HEADS_H - 1
            turns(a)
            levels(0, a)
            levels(1, a)
            chunk_kv(a)
            levels(2, a)
            levels(3, a)
            outputs(a)
            output_sums(a)
            linear(S["gb"], DT, x_hi, x_lo, None, None)
            linear(S["upb"], DT, hid_hi, hid_lo, hid_low, HID_HEADS)
            linear(S["out1"], DT, hid_hi, hid_lo, hid_low, HID_MIX)

            def ff1(ch, first):
                p0 = S["ff1"] + 16 * ch
                for m in range(DT):
                    product(p0 + m, m, x_hi, x_lo, DT, x_low if first and m == 0 else None, 8 * X_FFN)
                    if first and m == 0:
                        stream_sums(S_FFN)
                for m in range(DT):
                    product(p0 + (8 + m), m, hid_hi, hid_lo, DT, hid_low if m == 0 else None,
                            8 * ch + HID_FF1)

            ff1(0, True)
            with pe.Fori(1, FF1_CHUNKS) as ch:
                ff1(ch, False)
            stream_sums(S_FINAL)

            linear(S["conv_b"], DT, x_hi, x_lo, x_low, 8 * X_ATTN0, stream=S_ATTN0)
            with pe.Fori(0, 4) as i:
                for j in range(4):
                    product(i * 4 + (S["conv_ch"] + j), S["conv_ch"] + j, x_hi, x_lo)
            linear(S["out2"], DT, hid_hi, hid_lo, hid_low, HID_CONV)

            def ffn(l):
                p0, t0 = S[f"ffn_{l}"], 0
                for n, size in enumerate(FF2_CHUNKS):
                    if n == 0:
                        linear(p0, 4, x_hi, x_lo, x_low, 8 * (X_FFN1 if l else X_FFN0),
                               stream=S_FFN1 if l else S_FFN0)
                    with pe.Fori(int(n == 0), size // 2) as i:
                        for j in range(4):
                            product(i * 4 + (p0 + j), p0 + j, x_hi, x_lo)
                    p0 += 2 * size
                    linear(p0, DT, hid_hi, hid_lo, hid_low, (HID_FFN1 if l else HID_FFN0) + t0, tiles=size)
                    p0 += DT
                    t0 += size

            ffn(0)

            def k_sums(m):
                pe.wait_ge(k_squared, m + 1)
                pe.wait_ge(var_ready, R_K + m)
                sums(7, c("halves"), k_sq[:, m % 2, :])

            def spread_v(m):
                pe.wait_ge(evicted, S["v"] + m + 1)
                if m >= 2:
                    pe.wait_ge(v_copied, m - 1)
                for b in range(BLK):
                    ins = nc.tensor.transpose(ps[:, 2 + m % 2, b * P:(b + 1) * P],
                                              v_raw[:, m % 2, b * P:(b + 1) * P], c("ident"))
                ins.then_inc(v_spread, 1)

            for m in range(DT):
                product(S["k"] + m, S["k"] + m, x_hi, x_lo, DT, x_low if m == 0 else None, 8 * X_KV)
                if m == 0:
                    stream_sums(S_ATTN1)
                if m > 0:
                    k_sums(m - 1)
            for m in range(DT):
                product(S["v"] + m, S["v"] + m, x_hi, x_lo)
                if m == 0:
                    k_sums(DT - 1)
                if m > 0:
                    spread_v(m - 1)
            product(S["f"], S["f"], x_hi, x_lo)
            spread_v(DT - 1)

            SC = [(3, 384), (4, 0), (3, 0), (2, 0)]

            def score(a, side):
                r = slice(side * HEAD_DIM, (side + 1) * HEAD_DIM)
                for b in (3, 2, 0, 1):
                    n = P * (b + 1)
                    bk, at = SC[b]
                    nc.tensor.matmul(ps[:, bk, at:at + n], q_n[r, b * P:(b + 1) * P], k_now[r, 0:n],
                                     start=True, stop=False)
                    ins = nc.tensor.matmul(ps[:, bk, at + n - P:at + n], identb[:, :], negb[:, :],
                                           start=False, stop=True)
                ins.then_inc(scored, 1)

            def turn_prob(t):
                for b in range(BLK):
                    if b == 0:
                        pe.wait_ge(scaled, t * BLK + BLK)
                    if b >= 2 or not isinstance(t, int) or t > 0:
                        pe.wait_ge(copied_odd if b % 2 else copied_even, t * 2 + b // 2)
                    for qb in range(b, BLK):
                        at = OFF_P[qb] + b * P
                        ins = nc.tensor.transpose(ps[:, 5 + b % 2, qb * P:(qb + 1) * P], prob[:, at:at + P], c("ident"))
                    ins.then_inc(turned_p, 1)

            def attend(t, side):
                pe.wait_ge(copied_even, t * 2 + 2)
                pe.wait_ge(copied_odd, t * 2 + 2)
                bk = 7 if side == 0 else 2
                for b in range(BLK):
                    ins = nc.tensor.matmul(ps[:, bk, b * P:SEQ], v_now[:, b * P:(b + 1) * P],
                                           prob_t[:, OFF_T[b]:OFF_T[b] + SEQ - P * b],
                                           start=(b == 0), stop=(b == BLK - 1))
                ins.then_inc(attended, 1)

            def pair(m, m_int, a):
                p = S["qg"] + 2 * m if m is not None else None
                if a is not None:
                    pe.wait_ge(picked, 2 * a + 1)
                    if not isinstance(a, int) or a > 0:
                        pe.wait_ge(attn_read, 2 * a)
                    nc.tensor.matmul(ps[:, 7, :], c("minus")[0:HEADS_A, :], log_pick[0:HEADS_A, :],
                                     start=True, stop=True).then_inc(biased, 1)
                    pe.wait_ge(q_normed, a + 1)
                    pe.wait_ge(head_loaded, 2 * a + 2)
                    score(a, 0)
                if m is not None:
                    product(p, S["qg"] + 2 * m_int, x_hi, x_lo, DT, x_low if isinstance(m, int) and m == 0 else None, 8 * X_Q)
                if a is not None:
                    turn_prob(2 * a)
                    pe.wait_ge(picked, 2 * a + 2)
                    pe.wait_ge(bias_read, 2 * a + 1)
                    nc.tensor.matmul(ps[:, 7, :], c("minus")[0:HEADS_A, :], log_pick[0:HEADS_A, :],
                                     start=True, stop=True).then_inc(biased, 1)
                    pe.wait_ge(maxed, a * (2 * BLK) + BLK)
                    score(a, 1)
                if m is not None:
                    product(p + 1, S["qg"] + 2 * m_int + 1, x_hi, x_lo)
                if a is not None:
                    pe.wait_ge(bias_read, 2 * a + 2)
                    attend(2 * a, 0)
                    turn_prob(2 * a + 1)
                if m is not None:
                    pe.wait_ge(q_squared, m + 1)
                    if a is not None:
                        pe.wait_ge(maxed, a * (2 * BLK) + 2 * BLK)
                    sums(3, c("halves"), q_sq[:, :])
                if a is not None:
                    pe.wait_ge(maxed, a * (2 * BLK) + 2 * BLK)
                    attend(2 * a + 1, 1)

            pair(0, 0, None)
            with pe.Fori(0, DT // 2 - 1) as i:
                for j in range(2):
                    pair(i * 2 + (j + 1), j + 1, i * 2 + j)
            pair(DT - 1, DT - 1, DT - 2)
            pair(None, None, DT - 1)
            linear(S["out3"], DT, hid_hi, hid_lo, hid_low, HID_ATTN)
            ffn(1)


def constants():
    t = np.arange(P)
    levels = np.zeros((P, LEVELS, P), np.float32)
    for n, half in enumerate(HALVES):
        same = t[:, None] // (2 * half) == t[None, :] // (2 * half)
        levels[:, n] = same & (t[:, None] % (2 * half) < half) & (t[None, :] % (2 * half) >= half)
    reset = np.tile((np.arange(SEQ) % P != 0).astype(np.float32), (P, 1))
    parts = {"ident": np.eye(P), "ones": np.ones((P, P)),
             "halves": (t[:, None] // HEAD_DIM == t[None, :] // HEAD_DIM),
             "minus": -np.ones((P, P)), "neg": np.where(t[None, :] > t[:, None], NEG, 0.0),
             "reset": reset, "levels": levels.reshape(P, -1), "onehot": np.eye(P)[:, :HEADS_A]}
    return np.concatenate([np.asarray(parts[n], np.float32) for n in CONST_COLS], axis=1)


def by_panel(w):
    rows, cols = w.shape
    out = np.zeros((cols // P, P, DT, P), w.dtype)
    out[:, :, :rows // P] = w.reshape(rows // P, P, cols // P, P).transpose(2, 1, 0, 3)
    return out.reshape(cols // P, P, D)


def lay_out(i):
    w_in = i["w_in"][0]
    g = GROUPS * P
    zu, zv, zq, zf, zi, zo, ga, gb = (by_panel(w) for w in np.split(w_in, np.cumsum(
        [g, g, D, D, D, D, D]).tolist(), axis=1))
    heads = np.stack([zf, zq, zi, zo], axis=1).reshape(-1, P, D)
    ff_up, ff_down = by_panel(i["w_ff1"][0]), i["w_ff2"][0]
    ff1 = []
    for ch in range(FF1_CHUNKS):
        ff1 += [ff_up[8 * ch:8 * ch + 8], by_panel(ff_down[D * ch:D * ch + D])]
    b, cc, hh = (by_panel(w) for w in np.split(i["a_w_in_2"][0], 3, axis=1))
    conv_ch = np.stack([cc, hh], axis=1).reshape(-1, P, D)

    def ffn(l):
        a, gg = (by_panel(w) for w in np.split(i["ffn_w_up_2"][l], 2, axis=1))
        out, t = [], 0
        for size in FF2_CHUNKS:
            out.append(np.stack([a[t:t + size], gg[t:t + size]], axis=1).reshape(-1, P, D))
            out.append(by_panel(i["ffn_w_down_2"][l][t * P:(t + size) * P]))
            t += size
        return np.concatenate(out)

    kvf = i["w_kvf_2"]
    forget = np.zeros((D, P), kvf.dtype)
    forget[:, :HEADS_A] = kvf[:, 2 * D:]
    qp, gp = (by_panel(w) for w in np.split(i["b_w_qg_2"][0], 2, axis=1))
    qg = np.stack([qp, gp], axis=1).reshape(-1, P, D)
    panels = np.concatenate([zu, zv, ga, by_panel(i["w_up_a"][0]), heads, gb, by_panel(i["w_up_b"][0]),
                             by_panel(i["w_out"][0]), *ff1, b, conv_ch, by_panel(i["a_w_out_2"][0]), ffn(0),
                             by_panel(kvf[:, :D]), by_panel(kvf[:, D:2 * D]), by_panel(forget), qg,
                             by_panel(i["b_w_out_2"][0]), ffn(1)])

    def cols(a):
        return a.reshape(-1, P).T

    b_f = np.zeros((P, 1), np.float32)
    b_f[:HEADS_A, 0] = i["b_f_2"]
    parts = {"norm_mix": cols(i["norm_mix"][0]), "norm_ffn": cols(i["norm_ffn"][0]),
             "final_norm": cols(i["final_norm"]), "attn_0": cols(i["attn_norm_2"][0]),
             "attn_1": cols(i["attn_norm_2"][1]), "ffn_0": cols(i["ffn_norm_2"][0]),
             "ffn_1": cols(i["ffn_norm_2"][1]), "kv": cols(i["kv_norm_2"]),
             "hg_norm": i["hg_norm_g"][0][:, None], "k_norm": np.tile(i["k_norm_2"], 2)[:, None],
             "q_norm": np.tile(i["q_norm_2"][0], 2)[:, None], "b_f": b_f,
             "a_conv": cols(i["a_conv_2"][0].reshape(-1)), "conv_0": cols(i["ffn_conv_2"][0].reshape(-1)),
             "conv_1": cols(i["ffn_conv_2"][1].reshape(-1))}
    param = np.concatenate([parts[n] for n in PARAM_COLS], axis=1)
    rows = np.stack([i["gmlp_ln_g"][0], i["gmlp_ln_b"][0], i["gmlp_bs"][0].reshape(-1)])
    ws = i["gmlp_ws"][0].transpose(2, 0, 1)
    xT = i["x"][0].T.reshape(DT, P, SEQ)
    return {"xT": xT, "panels": panels, "const": constants(), "param": param, "rows": rows, "ws": ws}


def kernel(**inputs):
    import concourse.bacc as bacc
    from concourse.bass_utils import run_bass_kernel_spmd

    nc = bacc.Bacc("TRN2", target_bir_lowering=False, num_devices=1)
    arrays, args = {}, []
    for name, a in lay_out({n: np.asarray(a) for n, a in inputs.items()}).items():
        a = np.ascontiguousarray(a)
        arrays[f"in_{name}"] = a
        args.append(nc.dram_tensor(f"in_{name}", a.shape, mybir.dt.from_np(a.dtype), kind="ExternalInput").ap())
    out = nc.dram_tensor("outT", (DT, P, SEQ), mybir.dt.float32, kind="ExternalOutput").ap()
    build(nc, *args, out)
    r = run_bass_kernel_spmd(nc, [arrays], core_ids=[0])
    return r.results[0]["outT"].reshape(1, D, SEQ).transpose(0, 2, 1)
```

```python
from contextlib import ExitStack, contextmanager

import numpy as np

import concourse.bass as bass
from concourse import mybir

P = 128
SEQ = 512
D = 1024
DT = D // P
GROUPS = 4
HEADS_H = 8
D_FF1 = 4 * D
FF1_CHUNKS = D_FF1 // D
D_FF2 = 2816
FF2_TILES = D_FF2 // P
FF2_CHUNKS = (8, 8, 6)
HEADS_A = 16
HEAD_DIM = 64
EPS = 1e-6
BLK = SEQ // P
HALVES = (64, 32, 16, 8, 4, 2, 1)
LEVELS = len(HALVES)
NEG = -1e30
ARENA = 17424

RING = 4
COUNTS = [("zu", 4), ("zv", 4), ("ga", 8), ("upa", 8), ("heads", 32), ("gb", 8), ("upb", 8), ("out1", 8),
          ("ff1", 64), ("conv_b", 8), ("conv_ch", 16), ("out2", 8), ("ffn_0", 68), ("k", 8), ("v", 8),
          ("f", 1), ("qg", 16), ("out3", 8), ("ffn_1", 68)]
START, N_PANELS = {}, 0
for _name, _n in COUNTS:
    START[_name] = N_PANELS
    N_PANELS += _n

CONST_COLS, PARAM_COLS = {}, {}
_at = 0
for _name, _n in [("ident", P), ("ones", P), ("halves", P), ("minus", P), ("neg", P), ("reset", SEQ),
                  ("levels", LEVELS * P), ("onehot", HEADS_A), ("eps", 1)]:
    CONST_COLS[_name] = (_at, _n)
    _at += _n
N_CONST = _at
_at = 0
for _name, _n in [("norm_mix", DT), ("norm_ffn", DT), ("final_norm", DT), ("attn_0", DT), ("attn_1", DT),
                  ("ffn_0", DT), ("ffn_1", DT), ("kv", DT), ("hg_norm", 1), ("k_norm", 1), ("q_norm", 1),
                  ("b_f", 1), ("a_conv", 3 * DT), ("conv_0", 3 * FF2_TILES), ("conv_1", 3 * FF2_TILES)]:
    PARAM_COLS[_name] = (_at, _n)
    _at += _n
N_PARAM = _at

R_MIX, R_HEAD, R_FFN, R_FINAL, R_ATTN0, R_FFN0, R_ATTN1, R_K, R_Q, R_FFN1 = 0, 1, 9, 10, 11, 12, 13, 14, 22, 30
S_MIX, S_FFN, S_FINAL, S_ATTN0, S_FFN0, S_ATTN1, S_FFN1 = range(7)
X_MIX, X_FFN, X_ATTN0, X_FFN0, X_KV, X_Q, X_FFN1 = range(7)
HID_GMLP, HID_HEADS, HID_MIX, HID_FF1, HID_CONV, HID_FFN0, HID_ATTN, HID_FFN1 = 0, 4, 12, 20, 52, 60, 82, 90


class Steps:

    def __init__(self, eng, sem):
        self.eng, self.sem, self.n, self.offset = eng, sem, 0, 0

    def done(self, ins):
        ins.then_inc(self.sem, 1)
        self.n += 1
        return ins

    def wait(self):
        self.eng.wait_ge(self.sem, self.n + self.offset)

    @contextmanager
    def loop(self, first, end, marks):
        before = self.n
        with self.eng.Fori(first, end) as i:
            self.offset = (i - first) * marks
            yield i
        self.offset = 0
        assert self.n - before == marks, f"the body marks {self.n - before} steps, not {marks}"
        self.n = before + (end - first) * marks


def tile_at(buf, i):
    if isinstance(i, int):
        return buf[:, i, :]
    return buf[:, bass.ds(i, 1), :].rearrange("p a n -> p (a n)")


def column(buf, i, rows=P):
    return buf[0:rows, i:i + 1] if isinstance(i, int) else buf[0:rows, bass.ds(i, 1)]


def build(nc, xT, panels, const, param, rows, ws, outT):
    F, R, BF = mybir.dt.float32, mybir.dt.float32r, mybir.dt.bfloat16
    ALU = mybir.AluOpType
    ACT = mybir.ActivationFunctionType

    ctx = ExitStack()
    with ctx:
        def sb(name, shape, dt=F):
            return ctx.enter_context(nc.sbuf_tensor(name, shape, dt))

        def sem(name):
            return ctx.enter_context(nc.semaphore(name))

        w_raw = sb("w_raw", [P, RING, D])
        w_hi = sb("w_hi", [P, RING, D], R)
        w_lo = sb("w_lo", [P, RING, D], R)
        x = sb("x", [P, DT, SEQ])
        x_hi = sb("x_hi", [P, DT, SEQ], R)
        x_lo = sb("x_lo", [P, DT, SEQ], R)
        hid_hi = sb("hid_hi", [P, DT, SEQ], R)
        hid_lo = sb("hid_lo", [P, DT, SEQ], R)
        consts = sb("consts", [P, N_CONST])
        params = sb("params", [P, N_PARAM])
        identb = sb("identb", [P, P], BF)
        negb = sb("negb", [P, P], BF)
        wait_mark = sb("wait_mark", [P, 1])
        q_gain = sb("q_gain", [P, 1])
        inv_rms = sb("inv_rms", [P, SEQ])
        arena = sb("arena", [P, ARENA])

        def c(name):
            a, n = CONST_COLS[name]
            return consts[:, a:a + n]

        def gain(name, i=0):
            a, _ = PARAM_COLS[name]
            return column(params, a + i)

        used = [0]

        def take(*shape):
            n = int(np.prod(shape))
            a = used[0]
            used[0] += n
            assert used[0] <= ARENA, used[0]
            v = arena[:, a:a + n]
            if len(shape) == 2:
                v = v.rearrange("p (a n) -> p a n", a=shape[0])
            return v

        squares = take(2, SEQ)
        sum_sq = take(SEQ)
        o_sq, o_inv, o_tmp = squares[:, 0, :], squares[:, 1, :], sum_sq
        common = used[0]
        y = take(DT, SEQ)
        after_y = used[0]
        zu, zv = take(GROUPS, SEQ), take(GROUPS, SEQ)
        vn = take(BLK, SEQ)
        rows_sb = take(3, SEQ)
        ws_sb = take(GROUPS, P)
        ln_stats, ln_mv = take(BLK, 6), take(BLK, 2)
        ln_root, ln_inv = take(BLK), take(BLK)
        used[0] = after_y
        qk = take(2 + LEVELS, SEQ)
        masked = take(LEVELS + 1, P)
        at = used[0]
        z, za, g, cum = take(SEQ), take(SEQ), take(SEQ), take(SEQ)
        q, k, vT, silu_o = take(SEQ), take(SEQ), take(SEQ), take(SEQ)
        gb = arena[:, at:used[0]].rearrange("p (a n) -> p a n", a=DT)
        z_o = take(SEQ)
        v_nat, k_nat, scores = take(BLK, P), take(BLK - 1, P), take(BLK, P)
        state = k_nat
        chunk_decay = take(BLK)
        used[0] = after_y
        gy = take(2, SEQ)
        used[0] = after_y
        relu = take(2, SEQ)
        relu_sq = take(2, SEQ)
        used[0] = common
        conv_b = take(DT, SEQ)
        padded = take(2, SEQ + 2)
        conv_c, conv_t, conv_u, conv_o = take(2, SEQ), take(2, SEQ), take(2, SEQ), take(2, SEQ)
        used[0] = common
        k_all, v_all = take(DT, SEQ), take(DT, SEQ)
        attn_common = used[0]
        k_raw, v_raw, k_sq = take(2, SEQ), take(2, SEQ), take(2, SEQ)
        k_inv = take(SEQ)
        used[0] = attn_common
        OFF_P = [0, 128, 384, 768]
        OFF_T = [0, 512, 896, 1152]
        prob, prob_t = take(1280), take(1280)
        gate, gate_l = take(2, SEQ), take(SEQ)
        q_raw, q_n, q_sq = take(SEQ), take(SEQ), take(SEQ)
        q_inv = q_sq
        k_now, v_now, key_bias, o_all = take(SEQ), take(SEQ), take(SEQ), take(SEQ)
        log_c, log_pick = squares[:, 0, :], squares[:, 1, :]
        logit, logit_a = prob[:, 0:SEQ], prob[:, SEQ:2 * SEQ]
        row_max, row_neg, row_sum, row_inv = take(BLK), take(BLK), take(BLK), take(BLK)

        ps = ctx.enter_context(nc.psum_tensor("ps", [P, 8, SEQ], F))

        w_in = [sem(f"w_in{i}") for i in range(RING)]
        w_high, w_low = sem("w_high"), sem("w_low")
        made = sem("made")
        evicted = sem("evicted")
        x_in, c_in, row_in, out_done = sem("x_in"), sem("c_in"), sem("row_in"), sem("out_done")
        consts_ok = sem("consts_ok")
        x_high, x_low = sem("x_high"), sem("x_low")
        hid_high, hid_low = sem("hid_high"), sem("hid_low")
        squared, summed = sem("squared"), sem("summed")
        sums_ready, sums_read, root_ready = sem("sums_ready"), sem("sums_read"), sem("root_ready")
        x_final = sem("x_final")
        dve_steps, act_steps, pool_steps = sem("dve_steps"), sem("act_steps"), sem("pool_steps")
        gelu_done, v_turned, ln_var, ln_rooted, v_normed = (sem(n) for n in (
            "gelu_done", "v_turned", "ln_var", "ln_rooted", "v_normed"))
        mixed, mixed_read, y_a, ws_masked = sem("mixed"), sem("mixed_read"), sem("y_a"), sem("ws_masked")
        gate_a, gate_b, y_mixed = sem("gate_a"), sem("gate_b"), sem("y_mixed")
        f_log, f_k, k_done, q_log, q_arg, q_sig, q_done, o_log, o_arg, o_sig, o_gate = (sem(n) for n in (
            "f_log", "f_k", "k_done", "q_log", "q_arg", "q_sig", "q_done", "o_log", "o_arg", "o_sig", "o_gate"))
        turned_v, turned_k, diag_made, copied_v, copied_k = (sem(n) for n in (
            "turned_v", "turned_k", "diag_made", "copied_v", "copied_k"))
        level_made, level_masked, scores_done, kv_made, states_done = (sem(n) for n in (
            "level_made", "level_masked", "scores_done", "kv_made", "states_done"))
        spans_done, decays_done, keys_decayed, queries_decayed = (sem(n) for n in (
            "spans_done", "decays_done", "keys_decayed", "queries_decayed"))
        o_made, o_squared, y_b, cum_done = sem("o_made"), sem("o_squared"), sem("y_b"), sem("cum_done")
        relu_done, conv_done, silu_done, hid_raw = (sem(n) for n in (
            "relu_done", "conv_done", "silu_done", "hid_raw"))
        k_squared, k_normed, v_copied, v_flat, v_spread = (sem(n) for n in (
            "k_squared", "k_normed", "v_copied", "v_flat", "v_spread"))
        l_abs, l_log, l_done, picked, biased, bias_read = (sem(n) for n in (
            "l_abs", "l_log", "l_done", "picked", "biased", "bias_read"))
        k_loaded, v_loaded, scored, maxed, exped, scaled, turned_p, copied_even, copied_odd, attended, attn_read = (sem(n) for n in (
            "k_loaded", "v_loaded", "scored", "maxed", "exped", "scaled", "turned_p", "copied_even", "copied_odd", "attended", "attn_read"))
        q_squared, q_normed, gate_log, gate_arg, gate_done = (sem(n) for n in (
            "q_squared", "q_normed", "gate_log", "gate_arg", "gate_done"))

        block = ctx.enter_context(nc.Block())

        S = START
        SC = [(3, 384), (4, 0), (3, 0), (2, 0)]
        SCORE_ORDER = (0, 2, 1, 3)
        SCORES_BEFORE = (2, 3, 3, 4)

        @block.sync
        def _(sp):
            def load(i, j):
                sp.dma_start(w_raw[:, j, :], panels[bass.ds(i * RING + j, 1)].rearrange("a p n -> p (a n)")
                             if not isinstance(i, int) else panels[i * RING + j]).then_inc(w_in[j], 16)

            sp.dma_start(consts[:], const).then_inc(c_in, 16)
            sp.dma_start(params[:], param).then_inc(c_in, 16)
            for m in range(DT):
                sp.dma_start(x[:, m, :], xT[m]).then_inc(x_in, 16)
            for j in range(RING):
                load(0, j)
            sp.dma_start(rows_sb[:, :, :], rows.partition_broadcast(P)).then_inc(row_in, 16)
            sp.dma_start(ws_sb[:, :, :], ws).then_inc(row_in, 16)
            with sp.Fori(1, N_PANELS // RING) as i:
                at = sp.snap(i * RING)
                for j in range(RING):
                    src = panels[bass.ds(at + j, 1)].rearrange("a p n -> p (a n)")
                    sp.wait_ge(w_low, i * RING + (j - RING + 1))
                    sp.dma_start(w_raw[:, j, :], src).then_inc(w_in[j], 16)
            for pnl in range(N_PANELS - N_PANELS % RING, N_PANELS):
                sp.wait_ge(w_low, pnl - RING + 1)
                sp.dma_start(w_raw[:, pnl % RING, :], panels[pnl]).then_inc(w_in[pnl % RING], 16)
            for m in range(DT):
                sp.wait_ge(evicted, N_PANELS - DT + m + 1)
                sp.dma_start(outT[m], x[:, m, :]).then_inc(out_done, 16)
            sp.wait_ge(out_done, 16 * DT)

        @block.gpsimd
        def _(pool):
            steps = Steps(pool, pool_steps)

            def low(p, j):
                if isinstance(p, int) and p >= N_PANELS:
                    return
                pool.wait_ge(w_high, p + 1)
                if not isinstance(p, int) or p >= RING:
                    pool.wait_ge(made, p - RING + 1)
                nc.gpsimd.tensor_tensor(w_lo[:, j, :], w_raw[:, j, :], w_hi[:, j, :].bitcast(F),
                                        ALU.subtract).then_inc(w_low, 1)

            first = S["heads"] + 3
            for p in range(RING):
                low(p, p)
            with pool.Fori(1, first // RING) as i:
                for j in range(RING):
                    low(i * RING + j, j)
            for p in range(first - first % RING, first):
                low(p, p % RING)

            def chunk_scores(c_, a):
                pool.wait_ge(level_masked, a * BLK + (c_ + 1))
                steps.done(nc.gpsimd.tensor_tensor(masked[:, 0:4, :], masked[:, 0:4, :], masked[:, 4:8, :], ALU.add))
                steps.wait()
                steps.done(nc.gpsimd.tensor_tensor(masked[:, 0:2, :], masked[:, 0:2, :], masked[:, 2:4, :], ALU.add))
                steps.wait()
                if not isinstance(a, int) or a > 0:
                    pool.wait_ge(o_made, a)
                nc.gpsimd.tensor_tensor(scores[:, c_, :], masked[:, 0, :], masked[:, 1, :],
                                        ALU.add).then_inc(scores_done, 1)

            def decay_keys(h, tiles):
                for n in tiles:
                    if n == 0:
                        pool.wait_ge(k_done, h + 1)
                        nc.gpsimd.tensor_tensor(qk[:, 0, :], qk[:, 0, :], k[:, :], ALU.mult).then_inc(keys_decayed, 1)
                        continue
                    half = HALVES[n - 1]
                    lv = qk[:, 1 + n, :].rearrange("p (b s h) -> p b s h", s=2, h=half)[:, :, 0, :]
                    kv = k[:, :].rearrange("p (b s h) -> p b s h", s=2, h=half)[:, :, 0, :]
                    nc.gpsimd.tensor_tensor(lv, lv, kv, ALU.mult).then_inc(keys_decayed, 1)

            def head(h, a):
                p = S["heads"] + 4 * h if h is not None else S["gb"]
                low(p + 3, 3)
                if a is not None:
                    chunk_scores(0, a)
                    chunk_scores(1, a)
                low(p + 4, 0)
                if a is not None:
                    chunk_scores(2, a)
                    chunk_scores(3, a)
                low(p + 5, 1)
                if h is not None:
                    pool.wait_ge(decays_done, h * 4 + 1)
                    decay_keys(h, [0])
                low(p + 6, 2)
                if h is not None:
                    pool.wait_ge(decays_done, h * 4 + 2)
                    decay_keys(h, [1, 2, 3, 4])
                    pool.wait_ge(decays_done, h * 4 + 3)
                    decay_keys(h, [5, 6, 7])

            head(0, None)
            with steps.loop(1, HEADS_H, 2 * BLK) as h:
                head(h, h - 1)
            head(None, HEADS_H - 1)
            rest = S["gb"] + 7
            n = (N_PANELS - rest) // RING
            with pool.Fori(0, n) as i:
                for j in range(RING):
                    low(i * RING + (rest + j), (rest + j) % RING)
            for p in range(rest + n * RING, N_PANELS):
                low(p, p % RING)

        @block.scalar
        def _(act):
            steps = Steps(act, act_steps)

            def high(p, p_int):
                if isinstance(p, int) and p >= N_PANELS:
                    return
                j = p_int % RING
                act.wait_ge(w_in[j], panel_loads(p, p_int))
                if not isinstance(p, int) or p >= RING:
                    act.wait_ge(made, p - RING + 1)
                nc.scalar.copy(w_hi[:, j, :], w_raw[:, j, :]).then_inc(w_high, 1)

            def panel_loads(p, p_int):
                if isinstance(p, int):
                    return 16 * (p // RING + 1)
                return p * 4 + (16 - 4 * (p_int % RING))

            def split(dst, src, scale=None):
                return nc.scalar.activation(dst, src, ACT.Copy, scale=1.0 if scale is None else scale)

            def root(r, bank_n, inv_n, dst):
                act.wait_ge(sums_ready, r + 1)
                nc.scalar.activation(dst, ps[:, bank_n, :], ACT.Ln, bias=c("eps"), scale=inv_n).then_inc(sums_read, 1)
                act.wait_ge(sums_read, r + 1)
                nc.scalar.activation(dst, dst, ACT.Exp, scale=-0.5).then_inc(root_ready, 1)

            def stream_root(r):
                root(r, 7, 1.0 / D, inv_rms[:, :])

            def log_sigmoid_part(dst, src, done):
                steps.done(nc.scalar.activation(dst, src, ACT.Abs))
                steps.wait()
                steps.done(nc.scalar.activation(dst, dst, ACT.Exp, scale=-1.0))
                steps.wait()
                nc.scalar.activation(dst, dst, ACT.Ln, bias=1.0).then_inc(done, 1)

            def square_x(s, m):
                if s > 0 or m >= 2:
                    act.wait_ge(summed, 8 * s + m - 1)
                nc.scalar.activation(squares[:, m % 2, :], x[:, m, :], ACT.Square).then_inc(squared, 1)

            def split_x(m, name):
                split(x_hi[:, m, :], x[:, m, :], gain(name, m)).then_inc(x_high, 1)

            act.wait_ge(c_in, 32)
            for m in range(DT):
                act.wait_ge(x_in, 16 * DT)
                square_x(S_MIX, m)
                split_x(m, "norm_mix")
                if m < 3:
                    high(m, m)
            for m in range(8):
                high(m + 3, m + 3)
                if m == 0:
                    stream_root(R_MIX)
                t = zu[:, m, :] if m < 4 else zv[:, m - 4, :]
                act.wait_ge(evicted, m + 1)
                nc.scalar.activation(t, t, ACT.Gelu).then_inc(gelu_done, 1)
            def gate_ga(m):
                act.wait_ge(evicted, S["ga"] + m + 1)
                nc.scalar.activation(y[:, m, :], y[:, m, :], ACT.Sigmoid).then_inc(gate_a, 1)

            for m in range(DT):
                high(S["ga"] + m + 3, S["ga"] + m + 3)
                if m == 5:
                    act.wait_ge(ln_var, BLK)
                    steps.done(nc.scalar.activation(ln_root[:, :], ln_mv[:, :, 1], ACT.Ln, bias=c("eps")))
                    steps.wait()
                    nc.scalar.activation(ln_inv[:, :], ln_root[:, :], ACT.Exp, scale=-0.5).then_inc(ln_rooted, 1)
                    for n in range(m):
                        gate_ga(n)
                if m >= 5:
                    gate_ga(m)
            for gr in range(GROUPS):
                act.wait_ge(y_a, gr + 1)
                split(hid_hi[:, gr, :], zu[:, gr, :]).then_inc(hid_high, 1)
            for m in range(DT):
                high(S["upa"] + m + 3, S["upa"] + m + 3)

            def head(h, a):
                p = S["heads"] + 4 * h if h is not None else S["gb"]
                high(p + 3, S["heads"] + 3)
                if h is not None:
                    act.wait_ge(evicted, p + 1)
                    log_sigmoid_part(za[:, :], z[:, :], f_log)
                if a is not None:
                    act.wait_ge(turned_v, a + 1)
                    nc.scalar.copy(v_nat[:, :, :], ps[:, 2, :].rearrange("p (b n) -> p b n", b=BLK)).then_inc(copied_v, 1)
                    act.wait_ge(turned_k, a + 1)
                    nc.scalar.copy(k_nat[:, :, :], ps[:, 3, 0:384].rearrange("p (b n) -> p b n", b=BLK - 1)).then_inc(copied_k, 1)
                if h is not None:
                    act.wait_ge(f_k, h + 1)
                    if a is not None:
                        act.wait_ge(diag_made, a + 1)
                        act.wait_ge(keys_decayed, a * (LEVELS + 1) + (LEVELS + 1))
                    nc.scalar.activation(k[:, :], za[:, :], ACT.Exp).then_inc(k_done, 1)
                if a is not None:
                    act.wait_ge(o_arg, a + 1)
                    nc.scalar.activation(z_o[:, :], z_o[:, :], ACT.Exp).then_inc(o_sig, 1)
                high(p + 4, S["heads"] + 4)
                if h is not None:
                    act.wait_ge(evicted, p + 2)
                    act.wait_ge(k_done, h + 1)
                    log_sigmoid_part(za[:, :], z[:, :], q_log)
                high(p + 5, S["heads"] + 5)
                if h is not None:
                    act.wait_ge(q_arg, h + 1)
                    nc.scalar.activation(za[:, :], za[:, :], ACT.Exp).then_inc(q_sig, 1)
                    act.wait_ge(spans_done, h * 3 + 1)
                    nc.scalar.activation(qk[:, 0, :], qk[:, 0, :], ACT.Exp).then_inc(decays_done, 1)
                high(p + 6, S["heads"] + 6)
                if h is not None:
                    act.wait_ge(spans_done, h * 3 + 2)
                    nc.scalar.activation(qk[:, 2:6, :], qk[:, 2:6, :], ACT.Exp).then_inc(decays_done, 1)
                if a is not None:
                    act.wait_ge(o_made, a + 1)
                    nc.scalar.activation(o_sq[:, :], ps[:, 7, :], ACT.Square).then_inc(o_squared, 1)
                if h is not None:
                    act.wait_ge(spans_done, h * 3 + 3)
                    nc.scalar.activation(qk[:, 6:, :], qk[:, 6:, :], ACT.Exp).then_inc(decays_done, 1)
                    nc.scalar.activation(qk[:, 1, :], cum[:, :], ACT.Exp)
                    nc.scalar.activation(chunk_decay[:, :], cum[:, P - 1:SEQ:P], ACT.Exp).then_inc(decays_done, 1)
                if a is not None:
                    root(R_HEAD + a, 2, 1.0 / P, o_inv[:, :])
                if h is not None:
                    act.wait_ge(evicted, p + 4)
                    log_sigmoid_part(z_o[:, :], silu_o[:, :], o_log)
                if a is not None:
                    act.wait_ge(y_b, a + 1)
                    split(tile_at(hid_hi, a), o_tmp[:, :]).then_inc(hid_high, 1)

            head(0, None)
            with steps.loop(1, HEADS_H, 6) as h:
                head(h, h - 1)
            head(None, HEADS_H - 1)
            for m in range(DT):
                if m > 3:
                    high(S["gb"] + m + 3, S["gb"] + m + 3)
                act.wait_ge(evicted, S["gb"] + m + 1)
                nc.scalar.activation(gb[:, m, :], gb[:, m, :], ACT.Sigmoid).then_inc(gate_b, 1)
            for m in range(DT):
                high(S["upb"] + m + 3, S["upb"] + m + 3)
            for m in range(DT):
                act.wait_ge(y_mixed, m + 1)
                act.wait_ge(made, S["out1"])
                split(hid_hi[:, m, :], y[:, m, :]).then_inc(hid_high, 1)

            def residual(p0, s, name, feed=3):
                for m in range(DT):
                    high(p0 + m + feed, p0 + m + feed)
                    act.wait_ge(evicted, p0 + m + 1)
                    square_x(s, m)
                    if name:
                        split_x(m, name)

            residual(S["out1"], S_FFN, "norm_ffn")

            def ff1_up(ch, first):
                p0 = S["ff1"] + 16 * ch
                for m in range(DT):
                    high(p0 + m + 3, S["ff1"] + m + 3)
                    if first and m == 0:
                        stream_root(R_FFN)
                    act.wait_ge(hid_raw, 8 * ch + (m + 1))
                    split(hid_hi[:, m, :], relu_sq[:, m % 2, :]).then_inc(hid_high, 1)

            def ff1_down(ch):
                for m in range(DT):
                    high(S["ff1"] + 16 * ch + (m + 11), S["ff1"] + m + 11)

            ff1_up(0, True)
            ff1_down(0)
            with act.Fori(1, FF1_CHUNKS - 1) as ch:
                ff1_up(ch, False)
                ff1_down(ch)
            ff1_up(FF1_CHUNKS - 1, False)
            residual(S["ff1"] + 16 * FF1_CHUNKS - 8, S_FINAL, None)

            stream_root(R_FINAL)
            for m in range(DT):
                act.wait_ge(x_final, m + 1)
                square_x(S_ATTN0, m)
                split_x(m, "attn_0")

            for m in range(DT):
                high(S["conv_b"] + m + 3, S["conv_b"] + m + 3)
                if m == 0:
                    stream_root(R_ATTN0)

            def conv_pair(m, m_int):
                p = S["conv_ch"] + 2 * m
                high(p + 3, S["conv_ch"] + 2 * m_int + 3)
                high(p + 4, S["conv_ch"] + 2 * m_int + 4)
                act.wait_ge(hid_raw, m + (8 * FF1_CHUNKS + 1))
                split(tile_at(hid_hi, m), conv_o[:, m_int % 2, :]).then_inc(hid_high, 1)

            with act.Fori(0, DT // 2) as i:
                for j in range(2):
                    conv_pair(i * 2 + j, j)
            residual(S["out2"], S_FFN0, "ffn_0")

            def ffn(l):
                base = S[f"ffn_{l}"]
                raw0 = 8 * FF1_CHUNKS + DT + l * FF2_TILES
                p0, t0 = base, 0
                for n, size in enumerate(FF2_CHUNKS):
                    def pair(m, m_int, first):
                        p = p0 + 2 * m
                        high(p + 3, p0 + 2 * m_int + 3)
                        if first:
                            stream_root(R_FFN1 if l else R_FFN0)
                        act.wait_ge(conv_done, m + (l * FF2_TILES + t0 + 1))
                        nc.scalar.activation(conv_u[:, m_int % 2, :], conv_u[:, m_int % 2, :],
                                             ACT.Silu).then_inc(silu_done, 1)
                        high(p + 4, p0 + 2 * m_int + 4)
                        act.wait_ge(hid_raw, m + (raw0 + t0 + 1))
                        split(tile_at(hid_hi, m), conv_o[:, m_int % 2, :]).then_inc(hid_high, 1)

                    pair(0, 0, n == 0)
                    pair(1, 1, False)
                    with act.Fori(1, size // 2) as i:
                        for j in range(2):
                            pair(i * 2 + j, j, False)
                    p0 += 2 * size
                    t0 += size
                    if n == len(FF2_CHUNKS) - 1 and l == 0:
                        residual(p0, S_ATTN1, "kv")
                    else:
                        for m in range(DT):
                            high(p0 + m + 3, p0 + m + 3)
                    p0 += DT

            ffn(0)

            def root_k(m):
                if m > 0:
                    act.wait_ge(k_normed, m)
                root(R_K + m, 7, 1.0 / HEAD_DIM, k_inv[:, :])

            for m in range(DT):
                high(S["k"] + m + 3, S["k"] + m + 3)
                if m == 0:
                    stream_root(R_ATTN1)
                act.wait_ge(evicted, S["k"] + m + 1)
                nc.scalar.activation(k_sq[:, m % 2, :], k_raw[:, m % 2, :], ACT.Square).then_inc(k_squared, 1)
                if m > 0:
                    root_k(m - 1)
            for m in range(DT):
                high(S["v"] + m + 3, S["v"] + m + 3)
                if m == 0:
                    root_k(DT - 1)
                act.wait_ge(v_spread, m + 1)
                nc.scalar.copy(v_all[:, m, :], ps[:, 2 + m % 2, :]).then_inc(v_copied, 1)
            high(S["f"] + 3, S["f"] + 3)
            for m in range(DT):
                act.wait_ge(made, S["qg"])
                split_x(m, "attn_1")
            rows16 = slice(0, HEADS_A)
            act.wait_ge(l_abs, 1)
            steps.done(nc.scalar.activation(logit_a[rows16, :], logit_a[rows16, :], ACT.Exp, scale=-1.0))
            steps.wait()
            nc.scalar.activation(logit_a[rows16, :], logit_a[rows16, :], ACT.Ln, bias=1.0).then_inc(l_log, 1)

            def copy_bias(t):
                act.wait_ge(biased, t + 1)
                nc.scalar.copy(key_bias[:, :], ps[:, 7, :]).then_inc(bias_read, 1)

            def softmax(t):
                for b in range(BLK):
                    act.wait_ge(maxed, t * BLK + (b + 1))
                    at = prob[:, OFF_P[b]:OFF_P[b] + P * (b + 1)]
                    ins = nc.scalar.activation(at, at, ACT.Exp, bias=row_neg[:, b:b + 1],
                                               accum_out=row_sum[:, b:b + 1])
                ins.then_inc(exped, 1)

            def copy_prob(t, t_int):
                for b in (0, 2):
                    act.wait_ge(turned_p, t * BLK + (b + 1))
                    nc.scalar.copy(prob_t[:, OFF_T[b]:OFF_T[b] + SEQ - P * b],
                                   ps[:, 5 + b % 2, P * b:SEQ]).then_inc(copied_even, 1)

            def pair(m, m_int, a):
                p = S["qg"] + 2 * m if m is not None else None
                if m is not None:
                    high(p + 3, S["qg"] + 2 * m_int + 3)
                if a is not None:
                    softmax(2 * a)
                    if not isinstance(a, int) or a > 0:
                        act.wait_ge(attended, 2 * a)
                    nc.scalar.copy(v_now[:, :], tile_at(v_all, a)).then_inc(v_loaded, 1)
                if m is not None:
                    act.wait_ge(evicted, p + 1)
                    nc.scalar.activation(q_sq[:, :], q_raw[:, :], ACT.Square).then_inc(q_squared, 1)
                if a is not None:
                    copy_prob(2 * a, 0)
                    copy_bias(2 * a + 1)
                if m is not None:
                    high(p + 4, S["qg"] + 2 * m_int + 4)
                if a is not None:
                    softmax(2 * a + 1)
                if m is not None:
                    root(R_Q + m, 7, 1.0 / HEAD_DIM, q_inv[:, :])
                    if a is not None:
                        act.wait_ge(scored, a * (2 * BLK) + 2 * BLK)
                    nc.scalar.copy(k_now[:, :], tile_at(k_all, m)).then_inc(k_loaded, 1)
                    act.wait_ge(evicted, p + 2)
                    log_sigmoid_part(gate_l[:, :], gate[:, m_int % 2, :], gate_log)
                    act.wait_ge(gate_arg, m + 1)
                    nc.scalar.activation(gate[:, m_int % 2, :], gate_l[:, :], ACT.Exp).then_inc(gate_done, 1)
                if a is not None:
                    copy_prob(2 * a + 1, 1)
                if m is not None:
                    copy_bias(2 * m)
                if a is not None:
                    act.wait_ge(attn_read, 2 * a + 2)
                    split(tile_at(hid_hi, a), o_all[:, :]).then_inc(hid_high, 1)

            pair(0, 0, None)
            with steps.loop(0, DT // 2 - 1, 2 * 2) as i:
                pair(i * 2 + 1, 1, i * 2)
                pair(i * 2 + 2, 2, i * 2 + 1)
            pair(DT - 1, DT - 1, DT - 2)
            high(S["out3"] + 3, S["out3"] + 3)
            pair(None, None, DT - 1)
            for m in range(DT):
                if m > 0:
                    high(S["out3"] + m + 3, S["out3"] + m + 3)
                act.wait_ge(evicted, S["out3"] + m + 1)
                square_x(S_FFN1, m)
                split_x(m, "ffn_1")
            ffn(1)

        @block.vector
        def _(dve):
            v = nc.vector
            steps = Steps(dve, dve_steps)

            def link(ins):
                steps.done(ins)
                steps.wait()

            def bank(p_int):
                return ps[:, p_int % 2, :]

            def wait_made(p):
                dve.wait_ge(made, p + 1)

            def scale_out(dst, p, p_int):
                wait_made(p)
                return v.tensor_tensor(dst, bank(p_int), inv_rms[:, :], ALU.mult)

            def wait_root(r):
                dve.wait_ge(root_ready, r + 1)

            def sum_squares(s, m):
                dve.wait_ge(squared, 8 * s + m + 1)
                if m == 0:
                    v.tensor_copy(sum_sq[:, :], squares[:, 0, :]).then_inc(summed, 1)
                else:
                    dve.wait_ge(summed, 8 * s + m)
                    v.tensor_tensor(sum_sq[:, :], sum_sq[:, :], squares[:, m % 2, :], ALU.add).then_inc(summed, 1)

            def low_x(n, m, name):
                dve.wait_ge(x_high, 8 * n + m + 1)
                v.scalar_tensor_tensor(x_lo[:, m, :], x[:, m, :], gain(name, m), x_hi[:, m, :].bitcast(F),
                                       ALU.mult, ALU.subtract).then_inc(x_low, 1)

            def low_hid(count, m, src):
                dve.wait_ge(hid_high, count)
                v.tensor_tensor(tile_at(hid_lo, m), src, tile_at(hid_hi, m).bitcast(F),
                                ALU.subtract).then_inc(hid_low, 1)

            def residual(p0, s, n, name):
                for m in range(DT):
                    wait_made(p0 + m)
                    v.tensor_tensor(x[:, m, :], x[:, m, :], bank(p0 + m), ALU.add).then_inc(evicted, 1)
                    if s is not None:
                        sum_squares(s, m)
                    if name:
                        low_x(n, m, name)

            dve.wait_ge(c_in, 32)
            v.tensor_copy(identb[:, :], c("ident")).then_inc(consts_ok, 1)
            v.tensor_copy(negb[:, :], c("neg")).then_inc(consts_ok, 1)
            for m in range(DT):
                sum_squares(S_MIX, m)
                low_x(X_MIX, m, "norm_mix")
            dve.wait_ge(row_in, 32)
            v.memset(ws_sb[P // 2:P, :, 0:P // 2], 0.0).then_inc(ws_masked, 1)
            wait_root(R_MIX)
            for m in range(8):
                scale_out(zu[:, m, :] if m < 4 else zv[:, m - 4, :], m, m).then_inc(evicted, 1)
            lng, lnb, bs = rows_sb[:, 0, :], rows_sb[:, 1, :], rows_sb[:, 2, :]

            def layer_norm(b):
                link(v.tensor_scalar(vn[:, b, :], ps[:, 2 + b, :], ln_mv[:, b, 0:1], ln_inv[:, b:b + 1],
                                     ALU.subtract, ALU.mult))
                link(v.tensor_tensor(vn[:, b, :], vn[:, b, :], lng, ALU.mult))
                v.tensor_tensor(vn[:, b, :], vn[:, b, :], lnb, ALU.add).then_inc(v_normed, 1)

            for m in range(DT):
                scale_out(y[:, m, :], S["ga"] + m, m).then_inc(evicted, 1)
                if 1 <= m < 5:
                    b = m - 1
                    dve.wait_ge(v_turned, b + 1)
                    link(v.bn_stats(ln_stats[:, b, :], ps[:, 2 + b, :]))
                    v.bn_aggr(ln_mv[:, b, :], ln_stats[:, b, :]).then_inc(ln_var, 1)
                if m == 5:
                    dve.wait_ge(ln_rooted, 1)
                    layer_norm(0)
                    layer_norm(1)
                if m == 6:
                    layer_norm(2)
                    layer_norm(3)
            for gr in range(GROUPS):
                dve.wait_ge(mixed, gr + 1)
                bias = bs[:, gr * P:(gr + 1) * P].unsqueeze(1).broadcast_to([P, BLK, P])
                v.tensor_tensor(zv[:, gr, :].rearrange("p (b n) -> p b n", b=BLK),
                                ps[:, 2 + gr % 2, :].rearrange("p (b n) -> p b n", b=BLK),
                                bias, ALU.add).then_inc(mixed_read, 1)
                dve.wait_ge(mixed_read, gr + 1)
                v.tensor_tensor(zu[:, gr, :], zu[:, gr, :], zv[:, gr, :], ALU.mult).then_inc(y_a, 1)
                low_hid(HID_GMLP + gr + 1, gr, zu[:, gr, :])
            for m in range(DT):
                wait_made(S["upa"] + m)
                dve.wait_ge(gate_a, m + 1)
                v.tensor_tensor(y[:, m, :], y[:, m, :], bank(S["upa"] + m), ALU.mult).then_inc(evicted, 1)

            def mask_chunk(c_, a):
                dve.wait_ge(level_made, a * BLK + (c_ + 1))
                if c_ > 0 or not isinstance(a, int) or a > 0:
                    dve.wait_ge(scores_done, a * BLK + c_)
                lv = c("levels").rearrange("p (l n) -> p l n", l=LEVELS)
                v.tensor_tensor(masked[:, 0:4, :], ps[:, 4, :].rearrange("p (l n) -> p l n", l=4),
                                lv[:, 0:4, :], ALU.mult)
                v.tensor_tensor(masked[:, 4:LEVELS, :], ps[:, 5, 0:(LEVELS - 4) * P].rearrange("p (l n) -> p l n", n=P),
                                lv[:, 4:LEVELS, :], ALU.mult)
                v.tensor_tensor(masked[:, LEVELS, :], ps[:, 6, c_ * P:(c_ + 1) * P], c("ident"),
                                ALU.mult).then_inc(level_masked, 1)

            def states(a):
                dve.wait_ge(kv_made, a + 1)
                link(v.tensor_copy(state[:, 0, :], ps[:, 3, 0:P]))
                for n in range(1, BLK - 1):
                    ins = v.scalar_tensor_tensor(state[:, n, :], state[:, n - 1, :], chunk_decay[:, n:n + 1],
                                                 ps[:, 3, n * P:(n + 1) * P], ALU.mult, ALU.add)
                    if n < BLK - 2:
                        link(ins)
                ins.then_inc(states_done, 1)

            def span(n):
                if n == 0:
                    last = cum[:, P - 1:SEQ:P].unsqueeze(2).broadcast_to([P, BLK, P])
                    return v.tensor_tensor(qk[:, 0, :].rearrange("p (b n) -> p b n", b=BLK), last,
                                           cum[:, :].rearrange("p (b n) -> p b n", b=BLK), ALU.subtract)
                half = HALVES[n - 1]
                lv = qk[:, 1 + n, :].rearrange("p (b s h) -> p b s h", s=2, h=half)
                cu = cum[:, :].rearrange("p (b s h) -> p b s h", s=2, h=half)
                mid = cu[:, :, 0, half - 1:half].broadcast_to([P, SEQ // (2 * half), half])
                v.tensor_tensor(lv[:, :, 0, :], mid, cu[:, :, 0, :], ALU.subtract)
                return v.tensor_tensor(lv[:, :, 1, :], cu[:, :, 1, :], mid, ALU.subtract)

            def decay_queries(tiles):
                for n in tiles:
                    half = HALVES[n - 1]
                    lv = qk[:, 1 + n, :].rearrange("p (b s h) -> p b s h", s=2, h=half)[:, :, 1, :]
                    qv = q[:, :].rearrange("p (b s h) -> p b s h", s=2, h=half)[:, :, 1, :]
                    v.tensor_tensor(lv, lv, qv, ALU.mult).then_inc(queries_decayed, 1)

            def head(h, a):
                p = S["heads"] + 4 * h if h is not None else S["gb"]
                p4 = S["heads"]
                if h is not None:
                    if a is not None:
                        dve.wait_ge(q_done, h)
                    scale_out(z[:, :], p, p4).then_inc(evicted, 1)
                    if a is not None:
                        dve.wait_ge(cum_done, h)
                    dve.wait_ge(f_log, h + 1)
                    link(v.scalar_tensor_tensor(g[:, :], z[:, :], 0.0, za[:, :], ALU.min, ALU.subtract))
                    v.tensor_tensor(za[:, :], g[:, :], z[:, :], ALU.subtract).then_inc(f_k, 1)
                else:
                    scale_out(gb[:, 0, :], p, p4).then_inc(evicted, 1)
                if a is not None:
                    mask_chunk(0, a)
                    dve.wait_ge(o_log, a + 1)
                    v.scalar_tensor_tensor(z_o[:, :], silu_o[:, :], 0.0, z_o[:, :], ALU.min,
                                           ALU.subtract).then_inc(o_arg, 1)
                if h is not None:
                    v.tensor_tensor_scan(cum[:, :], c("reset"), g[:, :], 0.0, ALU.mult, ALU.add).then_inc(cum_done, 1)
                if a is not None:
                    mask_chunk(1, a)
                    dve.wait_ge(o_sig, a + 1)
                    v.tensor_tensor(silu_o[:, :], silu_o[:, :], z_o[:, :], ALU.mult).then_inc(o_gate, 1)
                if h is not None:
                    dve.wait_ge(k_done, h + 1)
                    scale_out(z[:, :], p + 1, p4 + 1).then_inc(evicted, 1)
                else:
                    scale_out(gb[:, 1, :], p + 1, p4 + 1).then_inc(evicted, 1)
                if a is not None:
                    states(a)
                    mask_chunk(2, a)
                if h is not None:
                    dve.wait_ge(q_log, h + 1)
                    v.scalar_tensor_tensor(za[:, :], z[:, :], 0.0, za[:, :], ALU.min, ALU.subtract).then_inc(q_arg, 1)
                if a is not None:
                    mask_chunk(3, a)
                if h is not None:
                    dve.wait_ge(q_sig, h + 1)
                    if a is not None:
                        dve.wait_ge(diag_made, a + 1)
                    v.tensor_tensor(q[:, :], z[:, :], za[:, :], ALU.mult).then_inc(q_done, 1)
                    dve.wait_ge(cum_done, h + 1)
                    if a is not None:
                        dve.wait_ge(turned_k, a + 1)
                    span(0).then_inc(spans_done, 1)
                    for n in range(1, 4):
                        span(n)
                    span(4).then_inc(spans_done, 1)
                    if a is not None:
                        dve.wait_ge(turned_v, a + 1)
                    scale_out(vT[:, :], p + 2, p4 + 2).then_inc(evicted, 1)
                    for n in range(5, LEVELS):
                        span(n)
                    span(LEVELS).then_inc(spans_done, 1)
                    dve.wait_ge(q_done, h + 1)
                    dve.wait_ge(decays_done, h * 4 + 2)
                    decay_queries([1, 2, 3, 4])
                    dve.wait_ge(decays_done, h * 4 + 3)
                    decay_queries([5, 6, 7])
                else:
                    scale_out(gb[:, 2, :], p + 2, p4 + 2).then_inc(evicted, 1)
                if a is not None:
                    wait_root(R_HEAD + a)
                    link(v.scalar_tensor_tensor(o_tmp[:, :], ps[:, 7, :], gain("hg_norm"), o_inv[:, :],
                                                ALU.mult, ALU.mult))
                    dve.wait_ge(o_gate, a + 1)
                    v.tensor_tensor(o_tmp[:, :], o_tmp[:, :], silu_o[:, :], ALU.mult).then_inc(y_b, 1)
                if h is not None:
                    if a is not None:
                        dve.wait_ge(y_b, a + 1)
                    scale_out(silu_o[:, :], p + 3, p4 + 3).then_inc(evicted, 1)
                    dve.wait_ge(decays_done, h * 4 + 4)
                    v.tensor_tensor(qk[:, 1, :], qk[:, 1, :], q[:, :], ALU.mult).then_inc(queries_decayed, 1)
                else:
                    scale_out(gb[:, 3, :], p + 3, p4 + 3).then_inc(evicted, 1)
                if a is not None:
                    low_hid(a + (HID_HEADS + 1), a, o_tmp[:, :])

            head(0, None)
            with steps.loop(1, HEADS_H, 4) as h:
                head(h, h - 1)
            head(None, HEADS_H - 1)
            for m in range(4, DT):
                scale_out(gb[:, m, :], S["gb"] + m, m).then_inc(evicted, 1)
            for m in range(DT):
                wait_made(S["upb"] + m)
                dve.wait_ge(gate_b, m + 1)
                v.tensor_tensor(gy[:, m % 2, :], gb[:, m, :], bank(m), ALU.mult).then_inc(evicted, 1)
                dve.wait_ge(evicted, S["upb"] + m + 1)
                v.tensor_tensor(y[:, m, :], y[:, m, :], gy[:, m % 2, :], ALU.add).then_inc(y_mixed, 1)
            for m in range(DT):
                low_hid(HID_MIX + m + 1, m, y[:, m, :])
            residual(S["out1"], S_FFN, X_FFN, "norm_ffn")

            def ff1_up(ch, first):
                p0 = S["ff1"] + 16 * ch
                for m in range(DT):
                    if first and m == 0:
                        wait_root(R_FFN)
                    scale_out(relu[:, m % 2, :], p0 + m, m).then_inc(evicted, 1)
                    dve.wait_ge(evicted, p0 + (m + 1))
                    v.scalar_tensor_tensor(relu_sq[:, m % 2, :], relu[:, m % 2, :], 0.0, relu[:, m % 2, :],
                                           ALU.max, ALU.mult).then_inc(hid_raw, 1)
                    low_hid(8 * ch + (HID_FF1 + m + 1), m, relu_sq[:, m % 2, :])

            def ff1_down(ch):
                for m in range(DT):
                    wait_made(S["ff1"] + 16 * ch + (8 + m))
                    v.tensor_tensor(x[:, m, :], x[:, m, :], bank(m), ALU.add).then_inc(evicted, 1)

            ff1_up(0, True)
            ff1_down(0)
            with dve.Fori(1, FF1_CHUNKS - 1) as ch:
                ff1_up(ch, False)
                ff1_down(ch)
            ff1_up(FF1_CHUNKS - 1, False)
            residual(S["ff1"] + 16 * FF1_CHUNKS - 8, S_FINAL, None, None)
            wait_root(R_FINAL)
            for m in range(DT):
                v.scalar_tensor_tensor(x[:, m, :], x[:, m, :], gain("final_norm", m), inv_rms[:, :],
                                       ALU.mult, ALU.mult).then_inc(x_final, 1)
                sum_squares(S_ATTN0, m)
                low_x(X_ATTN0, m, "attn_0")

            v.memset(padded[:, :, 0:2], 0.0)
            wait_root(R_ATTN0)
            for m in range(DT):
                scale_out(conv_b[:, m, :], S["conv_b"] + m, S["conv_b"] + m).then_inc(evicted, 1)

            def convolve(dst, src, taps):
                link(v.tensor_scalar(dst, src[:, 2:SEQ + 2], taps[2], None, ALU.mult))
                link(v.scalar_tensor_tensor(dst, src[:, 1:SEQ + 1], taps[1], dst, ALU.mult, ALU.add))
                return v.scalar_tensor_tensor(dst, src[:, 0:SEQ], taps[0], dst, ALU.mult, ALU.add)

            def conv_pair(m, j):
                p = S["conv_ch"] + 2 * m
                scale_out(conv_c[:, j, :], p, S["conv_ch"]).then_inc(evicted, 1)
                scale_out(conv_t[:, j, :], p + 1, S["conv_ch"] + 1).then_inc(evicted, 1)
                dve.wait_ge(evicted, p + 2)
                link(v.tensor_tensor(padded[:, j, 2:SEQ + 2], conv_c[:, j, :], conv_t[:, j, :], ALU.mult))
                link(convolve(conv_u[:, j, :], padded[:, j, :], [gain("a_conv", m + t * DT) for t in range(3)]))
                v.tensor_tensor(conv_o[:, j, :], conv_u[:, j, :], tile_at(conv_b, m),
                                ALU.mult).then_inc(hid_raw, 1)
                low_hid(m + (HID_CONV + 1), m, conv_o[:, j, :])

            with steps.loop(0, DT // 2, 8) as i:
                for j in range(2):
                    conv_pair(i * 2 + j, j)
            residual(S["out2"], S_FFN0, X_FFN0, "ffn_0")

            def ffn(l):
                p0, t0 = S[f"ffn_{l}"], 0
                hid0 = HID_FFN1 if l else HID_FFN0
                v.memset(padded[:, :, 0:2], 0.0)
                wait_root(R_FFN1 if l else R_FFN0)
                for n, size in enumerate(FF2_CHUNKS):
                    def pair(m, j):
                        p = p0 + 2 * m
                        scale_out(padded[:, j, 2:SEQ + 2], p, p0).then_inc(evicted, 1)
                        dve.wait_ge(evicted, p + 1)
                        convolve(conv_u[:, j, :], padded[:, j, :],
                                 [gain(f"conv_{l}", m + (t * FF2_TILES + t0)) for t in range(3)]).then_inc(conv_done, 1)
                        scale_out(conv_t[:, j, :], p + 1, p0 + 1).then_inc(evicted, 1)
                        dve.wait_ge(evicted, p + 2)
                        dve.wait_ge(silu_done, m + (l * FF2_TILES + t0 + 1))
                        v.tensor_tensor(conv_o[:, j, :], conv_u[:, j, :], conv_t[:, j, :],
                                        ALU.mult).then_inc(hid_raw, 1)
                        low_hid(m + (hid0 + t0 + 1), m, conv_o[:, j, :])

                    pair(0, 0)
                    pair(1, 1)
                    with steps.loop(1, size // 2, 4) as i:
                        for j in range(2):
                            pair(i * 2 + j, j)
                    p0 += 2 * size
                    t0 += size
                    last = n == len(FF2_CHUNKS) - 1
                    if last and l == 0:
                        residual(p0, S_ATTN1, X_KV, "kv")
                    else:
                        for m in range(DT):
                            wait_made(p0 + m)
                            v.tensor_tensor(x[:, m, :], x[:, m, :], bank(p0 + m), ALU.add).then_inc(evicted, 1)
                    p0 += DT

            ffn(0)

            wait_root(R_ATTN1)

            def norm_k(m):
                wait_root(R_K + m)
                v.scalar_tensor_tensor(k_all[:, m, :], k_raw[:, m % 2, :], gain("k_norm"), k_inv[:, :],
                                       ALU.mult, ALU.mult).then_inc(k_normed, 1)

            for m in range(DT):
                if m >= 2:
                    dve.wait_ge(k_normed, m - 1)
                scale_out(k_raw[:, m % 2, :], S["k"] + m, S["k"] + m).then_inc(evicted, 1)
                if m > 0:
                    norm_k(m - 1)
            for m in range(DT):
                if m >= 2:
                    dve.wait_ge(v_spread, m - 1)
                scale_out(v_raw[:, m % 2, :], S["v"] + m, S["v"] + m).then_inc(evicted, 1)
                if m == 0:
                    norm_k(DT - 1)
            r16 = slice(0, HEADS_A)
            p = S["f"]
            wait_made(p)
            dve.wait_ge(v_spread, DT)
            dve.wait_ge(v_copied, DT)
            v.tensor_tensor(logit[r16, :], ps[r16, p % 2, :], inv_rms[r16, :], ALU.mult).then_inc(evicted, 1)
            dve.wait_ge(evicted, p + 1)
            b_at = PARAM_COLS["b_f"][0]
            link(v.tensor_scalar(logit[r16, :], logit[r16, :], params[r16, b_at:b_at + 1], None, ALU.add))
            v.scalar_tensor_tensor(logit_a[r16, :], logit[r16, :], -1.0, logit[r16, :], ALU.mult,
                                   ALU.max).then_inc(l_abs, 1)
            for m in range(DT):
                low_x(X_Q, m, "attn_1")
            v.tensor_scalar(q_gain[:, :], gain("q_norm"), HEAD_DIM ** -0.5, None, ALU.mult)
            dve.wait_ge(l_log, 1)
            link(v.scalar_tensor_tensor(logit[r16, :], logit[r16, :], 0.0, logit_a[r16, :], ALU.min, ALU.subtract))
            a1, _ = CONST_COLS["ones"]
            link(v.tensor_tensor_scan(log_c[r16, :], consts[r16, a1:a1 + 1].broadcast_to([HEADS_A, SEQ]), logit[r16, :], 0.0,
                                      ALU.mult, ALU.add))

            def pick(t):
                if not isinstance(t, int) or t > 0:
                    dve.wait_ge(biased, t)
                hot = CONST_COLS["onehot"][0]
                v.tensor_scalar(log_pick[r16, :], log_c[r16, :], column(consts, hot + t, HEADS_A), None,
                                ALU.mult).then_inc(picked, 1)


            def maxima(t):
                dve.wait_ge(bias_read, t + 1)
                if not isinstance(t, int) or t > 0:
                    dve.wait_ge(turned_p, t * BLK)
                for b in range(BLK):
                    dve.wait_ge(scored, t * BLK + SCORES_BEFORE[b])
                    v.memset(wait_mark[:, :], 0.0)
                    n = P * (b + 1)
                    bk, at = SC[b]
                    link(v.tensor_tensor_reduce(out=prob[:, OFF_P[b]:OFF_P[b] + n], in0=ps[:, bk, at:at + n],
                                                in1=key_bias[:, 0:n], scale=1.0, scalar=-3e38,
                                                op0=ALU.add, op1=ALU.max, accum_out=row_max[:, b:b + 1]))
                    v.tensor_scalar(row_neg[:, b:b + 1], row_max[:, b:b + 1], -1.0, None,
                                    ALU.mult).then_inc(maxed, 1)

            def scale_prob(t):
                dve.wait_ge(exped, t + 1)
                link(v.reciprocal(row_inv[:, :], row_sum[:, :]))
                for b in range(BLK):
                    at = prob[:, OFF_P[b]:OFF_P[b] + P * (b + 1)]
                    v.tensor_scalar(at, at, row_inv[:, b:b + 1], None, ALU.mult).then_inc(scaled, 1)

            def copy_prob(t):
                for b in (1, 3):
                    dve.wait_ge(turned_p, t * BLK + (b + 1))
                    v.tensor_copy(prob_t[:, OFF_T[b]:OFF_T[b] + SEQ - P * b],
                                  ps[:, 5 + b % 2, P * b:SEQ]).then_inc(copied_odd, 1)

            def take_output(t, side, par):
                rows_ = slice(side * HEAD_DIM, (side + 1) * HEAD_DIM)
                dve.wait_ge(attended, t + 1)
                bk = 7 if side == 0 else 2
                return v.tensor_tensor(o_all[rows_, :], ps[rows_, bk, :], gate[rows_, par, :], ALU.mult)

            def pair(m, par, a):
                p = S["qg"] + 2 * m if m is not None else None
                last_par = 1 - par if m is not None else 1
                if a is not None:
                    maxima(2 * a)
                    pick(2 * a + 1)
                    scale_prob(2 * a)
                if m is not None:
                    scale_out(q_raw[:, :], p, S["qg"]).then_inc(evicted, 1)
                if a is not None:
                    copy_prob(2 * a)
                    maxima(2 * a + 1)
                    scale_prob(2 * a + 1)
                if m is not None:
                    wait_root(R_Q + m)
                    v.scalar_tensor_tensor(q_n[:, :], q_raw[:, :], q_gain[:, :], q_inv[:, :],
                                           ALU.mult, ALU.mult).then_inc(q_normed, 1)
                    pick(2 * m)
                    scale_out(gate[:, par, :], p + 1, S["qg"] + 1).then_inc(evicted, 1)
                if a is not None:
                    dve.wait_ge(gate_done, a + 1)
                    take_output(2 * a, 0, last_par).then_inc(attn_read, 1)
                if m is not None:
                    dve.wait_ge(gate_log, m + 1)
                    v.scalar_tensor_tensor(gate_l[:, :], gate[:, par, :], 0.0, gate_l[:, :], ALU.min,
                                           ALU.subtract).then_inc(gate_arg, 1)
                if a is not None:
                    copy_prob(2 * a + 1)
                    take_output(2 * a + 1, 1, last_par).then_inc(attn_read, 1)
                    low_hid(a + (HID_ATTN + 1), a, o_all[:, :])

            pair(0, 0, None)
            with steps.loop(0, DT // 2 - 1, 2 * 10) as i:
                pair(i * 2 + 1, 1, i * 2)
                pair(i * 2 + 2, 0, i * 2 + 1)
            pair(DT - 1, 1, DT - 2)
            pair(None, None, DT - 1)
            residual(S["out3"], S_FFN1, X_FFN1, "ffn_1")
            ffn(1)

        @block.tensor
        def _(pe):
            def product(p, p_int, hi, lo, tiles=DT, ready=None, done=None, part=None):
                j = p_int % RING
                part = part or (0, tiles)
                if part[0] == 0:
                    pe.wait_ge(w_low, p + 1)
                    if not isinstance(p, int) or p >= 2:
                        pe.wait_ge(evicted, p - 1)
                for kt in range(*part):
                    if ready is not None:
                        pe.wait_ge(ready, done + (kt + 1))
                    wh, wl = w_hi[:, j, kt * P:(kt + 1) * P], w_lo[:, j, kt * P:(kt + 1) * P]
                    o = ps[:, p_int % 2, :]
                    nc.tensor.matmul(o, wh, hi[:, kt, :], start=(kt == 0), stop=False)
                    nc.tensor.matmul(o, wh, lo[:, kt, :], start=False, stop=False)
                    ins = nc.tensor.matmul(o, wl, hi[:, kt, :], start=False, stop=(kt == tiles - 1))
                if part[1] == tiles:
                    ins.then_inc(made, 1)

            def sums(bank_n, weights, src):
                nc.tensor.matmul(ps[:, bank_n, :], weights, src, start=True, stop=True).then_inc(sums_ready, 1)

            def stream_sums(s):
                pe.wait_ge(summed, 8 * s + 8)
                sums(7, c("ones"), sum_sq[:, :])

            def linear(p0, n, hi, lo, ready, done, tiles=DT, stream=None):
                for m in range(n):
                    product(p0 + m, p0 + m, hi, lo, tiles, ready if m == 0 else None, done)
                    if m == 0 and stream is not None:
                        stream_sums(stream)

            pe.wait_ge(consts_ok, 2)
            linear(S["zu"], 8, x_hi, x_lo, x_low, 8 * X_MIX, stream=S_MIX)

            def turn_zv(b):
                pe.wait_ge(gelu_done, 8)
                for gr in range(GROUPS):
                    ins = nc.tensor.transpose(ps[:, 2 + b, gr * P:(gr + 1) * P],
                                              zv[:, gr, b * P:(b + 1) * P], c("ident"))
                ins.then_inc(v_turned, 1)

            for m in range(DT):
                product(S["ga"] + m, S["ga"] + m, x_hi, x_lo)
                if 1 <= m < 5:
                    turn_zv(m - 1)
            pe.wait_ge(ws_masked, 1)
            for gr in range(GROUPS):
                pe.wait_ge(v_normed, BLK)
                if gr >= 2:
                    pe.wait_ge(mixed_read, gr - 1)
                for b in range(BLK):
                    ins = nc.tensor.matmul(ps[:, 2 + gr % 2, b * P:(b + 1) * P], vn[:, b, gr * P:(gr + 1) * P],
                                           ws_sb[:, gr, :], start=True, stop=True)
                ins.then_inc(mixed, 1)
            linear(S["upa"], DT, hid_hi, hid_lo, hid_low, HID_GMLP, tiles=GROUPS)

            def turns(a):
                pe.wait_ge(evicted, a * 4 + (S["heads"] + 3))
                if not isinstance(a, int) or a > 0:
                    pe.wait_ge(sums_read, a + (R_HEAD))
                for b in range(BLK):
                    ins = nc.tensor.transpose(ps[:, 2, b * P:(b + 1) * P], vT[:, b * P:(b + 1) * P], c("ident"))
                ins.then_inc(turned_v, 1)
                pe.wait_ge(keys_decayed, a * (LEVELS + 1) + 1)
                if not isinstance(a, int) or a > 0:
                    pe.wait_ge(states_done, a)
                for b in range(BLK - 1):
                    ins = nc.tensor.transpose(ps[:, 3, b * P:(b + 1) * P], qk[:, 0, b * P:(b + 1) * P], c("ident"))
                ins.then_inc(turned_k, 1)
                pe.wait_ge(q_done, a + 1)
                pe.wait_ge(k_done, a + 1)
                if not isinstance(a, int) or a > 0:
                    pe.wait_ge(level_masked, a * BLK)
                for b in range(BLK):
                    at = slice(b * P, (b + 1) * P)
                    ins = nc.tensor.matmul(ps[:, 6, at], k[:, at], q[:, at], start=True, stop=True)
                ins.then_inc(diag_made, 1)

            def levels(c_, a):
                if c_ == 0:
                    pe.wait_ge(keys_decayed, a * (LEVELS + 1) + (LEVELS + 1))
                    pe.wait_ge(queries_decayed, a * (LEVELS + 1) + LEVELS)
                if c_ > 0 or not isinstance(a, int) or a > 0:
                    pe.wait_ge(level_masked, a * BLK + c_)
                at = slice(c_ * P, (c_ + 1) * P)
                for n in range(LEVELS):
                    ins = nc.tensor.matmul(ps[:, 4 + n // 4, (n % 4) * P:(n % 4 + 1) * P], qk[:, 2 + n, at],
                                           qk[:, 2 + n, at], start=True, stop=True)
                ins.then_inc(level_made, 1)

            def chunk_kv(a):
                pe.wait_ge(copied_v, a + 1)
                pe.wait_ge(copied_k, a + 1)
                for b in range(BLK - 1):
                    ins = nc.tensor.matmul(ps[:, 3, b * P:(b + 1) * P], k_nat[:, b, :], v_nat[:, b, :],
                                           start=True, stop=True)
                ins.then_inc(kv_made, 1)

            def outputs(a):
                if not isinstance(a, int) or a > 0:
                    pe.wait_ge(y_b, a)
                pe.wait_ge(states_done, a + 1)
                pe.wait_ge(queries_decayed, a * (LEVELS + 1) + (LEVELS + 1))
                for b in range(BLK):
                    at = slice(b * P, (b + 1) * P)
                    pe.wait_ge(scores_done, a * BLK + (b + 1))
                    ins = nc.tensor.matmul(ps[:, 7, at], v_nat[:, b, :], scores[:, b, :], start=True, stop=(b == 0))
                    if b > 0:
                        ins = nc.tensor.matmul(ps[:, 7, at], state[:, b - 1, :], qk[:, 1, at], start=False, stop=True)
                ins.then_inc(o_made, 1)

            def output_sums(a):
                pe.wait_ge(o_squared, a + 1)
                sums(2, c("ones"), o_sq[:, :])

            def head(h, a):
                p, p4 = S["heads"] + 4 * h if h is not None else S["gb"], S["heads"]
                product(p, p4, x_hi, x_lo)
                if a is not None:
                    turns(a)
                    levels(0, a)
                product(p + 1, p4 + 1, x_hi, x_lo, part=(0, 4))
                if a is not None:
                    levels(1, a)
                product(p + 1, p4 + 1, x_hi, x_lo, part=(4, DT))
                if a is not None:
                    chunk_kv(a)
                    levels(2, a)
                product(p + 2, p4 + 2, x_hi, x_lo, part=(0, 4))
                if a is not None:
                    levels(3, a)
                product(p + 2, p4 + 2, x_hi, x_lo, part=(4, DT))
                product(p + 3, p4 + 3, x_hi, x_lo, part=(0, 4))
                if a is not None:
                    outputs(a)
                product(p + 3, p4 + 3, x_hi, x_lo, part=(4, DT))
                if a is not None:
                    output_sums(a)

            head(0, None)
            with pe.Fori(1, HEADS_H) as h:
                head(h, h - 1)
            head(None, HEADS_H - 1)
            linear(S["gb"] + 4, DT - 4, x_hi, x_lo, None, None)
            linear(S["upb"], DT, hid_hi, hid_lo, hid_low, HID_HEADS)
            linear(S["out1"], DT, hid_hi, hid_lo, hid_low, HID_MIX)

            def ff1(ch, first):
                p0 = S["ff1"] + 16 * ch
                for m in range(DT):
                    product(p0 + m, m, x_hi, x_lo, DT, x_low if first and m == 0 else None, 8 * X_FFN)
                    if first and m == 0:
                        stream_sums(S_FFN)
                for m in range(DT):
                    product(p0 + (8 + m), m, hid_hi, hid_lo, DT, hid_low if m == 0 else None,
                            8 * ch + HID_FF1)

            ff1(0, True)
            with pe.Fori(1, FF1_CHUNKS) as ch:
                ff1(ch, False)
            stream_sums(S_FINAL)

            linear(S["conv_b"], DT, x_hi, x_lo, x_low, 8 * X_ATTN0, stream=S_ATTN0)
            with pe.Fori(0, 4) as i:
                for j in range(4):
                    product(i * 4 + (S["conv_ch"] + j), S["conv_ch"] + j, x_hi, x_lo)
            linear(S["out2"], DT, hid_hi, hid_lo, hid_low, HID_CONV)

            def ffn(l):
                p0, t0 = S[f"ffn_{l}"], 0
                for n, size in enumerate(FF2_CHUNKS):
                    if n == 0:
                        linear(p0, 4, x_hi, x_lo, x_low, 8 * (X_FFN1 if l else X_FFN0),
                               stream=S_FFN1 if l else S_FFN0)
                    with pe.Fori(int(n == 0), size // 2) as i:
                        for j in range(4):
                            product(i * 4 + (p0 + j), p0 + j, x_hi, x_lo)
                    p0 += 2 * size
                    linear(p0, DT, hid_hi, hid_lo, hid_low, (HID_FFN1 if l else HID_FFN0) + t0, tiles=size)
                    p0 += DT
                    t0 += size

            ffn(0)

            def k_sums(m):
                pe.wait_ge(k_squared, m + 1)
                pe.wait_ge(sums_read, R_K + m)
                sums(7, c("halves"), k_sq[:, m % 2, :])

            def spread_v(m):
                pe.wait_ge(evicted, S["v"] + m + 1)
                if m >= 2:
                    pe.wait_ge(v_copied, m - 1)
                for b in range(BLK):
                    ins = nc.tensor.transpose(ps[:, 2 + m % 2, b * P:(b + 1) * P],
                                              v_raw[:, m % 2, b * P:(b + 1) * P], c("ident"))
                ins.then_inc(v_spread, 1)

            for m in range(DT):
                product(S["k"] + m, S["k"] + m, x_hi, x_lo, DT, x_low if m == 0 else None, 8 * X_KV)
                if m == 0:
                    stream_sums(S_ATTN1)
                if m > 0:
                    k_sums(m - 1)
            for m in range(DT):
                product(S["v"] + m, S["v"] + m, x_hi, x_lo)
                if m == 0:
                    k_sums(DT - 1)
                if m > 0:
                    spread_v(m - 1)
            product(S["f"], S["f"], x_hi, x_lo)
            spread_v(DT - 1)


            def score(a, side):
                r = slice(side * HEAD_DIM, (side + 1) * HEAD_DIM)
                for b in SCORE_ORDER:
                    n = P * (b + 1)
                    bk, at = SC[b]
                    if b == 3 and side == 0 and (not isinstance(a, int) or a > 0):
                        pe.wait_ge(attn_read, 2 * a)
                    nc.tensor.matmul(ps[:, bk, at:at + n], q_n[r, b * P:(b + 1) * P], k_now[r, 0:n],
                                     start=True, stop=False)
                    nc.tensor.matmul(ps[:, bk, at + n - P:at + n], identb[:, :], negb[:, :],
                                     start=False, stop=True).then_inc(scored, 1)

            def turn_prob(t):
                for b in range(BLK):
                    if b == 0:
                        pe.wait_ge(scaled, t * BLK + BLK)
                    if b >= 2 or not isinstance(t, int) or t > 0:
                        pe.wait_ge(copied_odd if b % 2 else copied_even, t * 2 + b // 2)
                    for qb in range(b, BLK):
                        at = OFF_P[qb] + b * P
                        ins = nc.tensor.transpose(ps[:, 5 + b % 2, qb * P:(qb + 1) * P], prob[:, at:at + P], c("ident"))
                    ins.then_inc(turned_p, 1)

            def attend(t, side):
                pe.wait_ge(copied_even, t * 2 + 2)
                pe.wait_ge(copied_odd, t * 2 + 2)
                bk = 7 if side == 0 else 2
                for b in range(BLK):
                    ins = nc.tensor.matmul(ps[:, bk, b * P:SEQ], v_now[:, b * P:(b + 1) * P],
                                           prob_t[:, OFF_T[b]:OFF_T[b] + SEQ - P * b],
                                           start=(b == 0), stop=(b == BLK - 1))
                ins.then_inc(attended, 1)

            def bias(t):
                pe.wait_ge(picked, t + 1)
                nc.tensor.matmul(ps[:, 7, :], c("minus")[0:HEADS_A, :], log_pick[0:HEADS_A, :],
                                 start=True, stop=True).then_inc(biased, 1)

            def pair(m, m_int, a):
                p, p_int = (S["qg"] + 2 * m, S["qg"] + 2 * m_int) if m is not None else (None, None)
                if a is not None:
                    pe.wait_ge(q_normed, a + 1)
                    pe.wait_ge(k_loaded, a + 1)
                    score(a, 0)
                if m is not None:
                    product(p, p_int, x_hi, x_lo, DT, x_low if isinstance(m, int) and m == 0 else None, 8 * X_Q)
                if a is not None:
                    turn_prob(2 * a)
                    pe.wait_ge(bias_read, 2 * a + 1)
                    bias(2 * a + 1)
                    pe.wait_ge(maxed, a * (2 * BLK) + BLK)
                    score(a, 1)
                if m is not None:
                    product(p + 1, p_int + 1, x_hi, x_lo, part=(0, 4))
                    if a is not None:
                        pe.wait_ge(bias_read, 2 * a + 2)
                    pe.wait_ge(q_squared, m + 1)
                    sums(7, c("halves"), q_sq[:, :])
                    product(p + 1, p_int + 1, x_hi, x_lo, part=(4, DT))
                if a is not None:
                    if m is not None:
                        pe.wait_ge(sums_read, m + (R_Q + 1))
                    else:
                        pe.wait_ge(bias_read, 2 * a + 2)
                    pe.wait_ge(v_loaded, a + 1)
                    attend(2 * a, 0)
                    turn_prob(2 * a + 1)
                if m is not None:
                    if a is not None:
                        pe.wait_ge(attn_read, 2 * a + 1)
                    else:
                        pe.wait_ge(sums_read, m + (R_Q + 1))
                    bias(2 * m)
                if a is not None:
                    pe.wait_ge(maxed, a * (2 * BLK) + 2 * BLK)
                    attend(2 * a + 1, 1)

            pair(0, 0, None)
            with pe.Fori(0, DT // 2 - 1) as i:
                for j in range(2):
                    pair(i * 2 + (j + 1), j + 1, i * 2 + j)
            pair(DT - 1, DT - 1, DT - 2)
            pair(None, None, DT - 1)
            linear(S["out3"], DT, hid_hi, hid_lo, hid_low, HID_ATTN)
            ffn(1)


def constants():
    t = np.arange(P)
    levels = np.zeros((P, LEVELS, P), np.float32)
    for n, half in enumerate(HALVES):
        same = t[:, None] // (2 * half) == t[None, :] // (2 * half)
        levels[:, n] = same & (t[:, None] % (2 * half) < half) & (t[None, :] % (2 * half) >= half)
    reset = np.tile((np.arange(SEQ) % P != 0).astype(np.float32), (P, 1))
    parts = {"ident": np.eye(P), "ones": np.ones((P, P)),
             "halves": (t[:, None] // HEAD_DIM == t[None, :] // HEAD_DIM),
             "minus": -np.ones((P, P)), "neg": np.where(t[None, :] > t[:, None], NEG, 0.0),
             "reset": reset, "levels": levels.reshape(P, -1), "onehot": np.eye(P)[:, :HEADS_A],
             "eps": np.full((P, 1), EPS)}
    return np.concatenate([np.asarray(parts[n], np.float32) for n in CONST_COLS], axis=1)


def by_panel(w):
    rows, cols = w.shape
    out = np.zeros((cols // P, P, DT, P), w.dtype)
    out[:, :, :rows // P] = w.reshape(rows // P, P, cols // P, P).transpose(2, 1, 0, 3)
    return out.reshape(cols // P, P, D)


def lay_out(i):
    w_in = i["w_in"][0]
    g = GROUPS * P
    zu, zv, zq, zf, zi, zo, ga, gb = (by_panel(w) for w in np.split(w_in, np.cumsum(
        [g, g, D, D, D, D, D]).tolist(), axis=1))
    heads = np.stack([zf, zq, zi, zo], axis=1).reshape(-1, P, D)
    ff_up, ff_down = by_panel(i["w_ff1"][0]), i["w_ff2"][0]
    ff1 = []
    for ch in range(FF1_CHUNKS):
        ff1 += [ff_up[8 * ch:8 * ch + 8], by_panel(ff_down[D * ch:D * ch + D])]
    b, cc, hh = (by_panel(w) for w in np.split(i["a_w_in_2"][0], 3, axis=1))
    conv_ch = np.stack([cc, hh], axis=1).reshape(-1, P, D)

    def ffn(l):
        a, gg = (by_panel(w) for w in np.split(i["ffn_w_up_2"][l], 2, axis=1))
        out, t = [], 0
        for size in FF2_CHUNKS:
            out.append(np.stack([a[t:t + size], gg[t:t + size]], axis=1).reshape(-1, P, D))
            out.append(by_panel(i["ffn_w_down_2"][l][t * P:(t + size) * P]))
            t += size
        return np.concatenate(out)

    kvf = i["w_kvf_2"]
    forget = np.zeros((D, P), kvf.dtype)
    forget[:, :HEADS_A] = kvf[:, 2 * D:]
    qp, gp = (by_panel(w) for w in np.split(i["b_w_qg_2"][0], 2, axis=1))
    qg = np.stack([qp, gp], axis=1).reshape(-1, P, D)
    panels = np.concatenate([zu, zv, ga, by_panel(i["w_up_a"][0]), heads, gb, by_panel(i["w_up_b"][0]),
                             by_panel(i["w_out"][0]), *ff1, b, conv_ch, by_panel(i["a_w_out_2"][0]), ffn(0),
                             by_panel(kvf[:, :D]), by_panel(kvf[:, D:2 * D]), by_panel(forget), qg,
                             by_panel(i["b_w_out_2"][0]), ffn(1)])

    def cols(a):
        return a.reshape(-1, P).T

    b_f = np.zeros((P, 1), np.float32)
    b_f[:HEADS_A, 0] = i["b_f_2"]
    parts = {"norm_mix": cols(i["norm_mix"][0]), "norm_ffn": cols(i["norm_ffn"][0]),
             "final_norm": cols(i["final_norm"]), "attn_0": cols(i["attn_norm_2"][0]),
             "attn_1": cols(i["attn_norm_2"][1]), "ffn_0": cols(i["ffn_norm_2"][0]),
             "ffn_1": cols(i["ffn_norm_2"][1]), "kv": cols(i["kv_norm_2"]),
             "hg_norm": i["hg_norm_g"][0][:, None], "k_norm": np.tile(i["k_norm_2"], 2)[:, None],
             "q_norm": np.tile(i["q_norm_2"][0], 2)[:, None], "b_f": b_f,
             "a_conv": cols(i["a_conv_2"][0].reshape(-1)), "conv_0": cols(i["ffn_conv_2"][0].reshape(-1)),
             "conv_1": cols(i["ffn_conv_2"][1].reshape(-1))}
    param = np.concatenate([parts[n] for n in PARAM_COLS], axis=1)
    rows = np.stack([i["gmlp_ln_g"][0], i["gmlp_ln_b"][0], i["gmlp_bs"][0].reshape(-1)])
    ws = i["gmlp_ws"][0].transpose(2, 0, 1)
    xT = i["x"][0].T.reshape(DT, P, SEQ)
    return {"xT": xT, "panels": panels, "const": constants(), "param": param, "rows": rows, "ws": ws}


def kernel(**inputs):
    import concourse.bacc as bacc
    from concourse.bass_utils import run_bass_kernel_spmd

    nc = bacc.Bacc("TRN2", target_bir_lowering=False, num_devices=1)
    arrays, args = {}, []
    for name, a in lay_out({n: np.asarray(a) for n, a in inputs.items()}).items():
        a = np.ascontiguousarray(a)
        arrays[f"in_{name}"] = a
        args.append(nc.dram_tensor(f"in_{name}", a.shape, mybir.dt.from_np(a.dtype), kind="ExternalInput").ap())
    out = nc.dram_tensor("outT", (DT, P, SEQ), mybir.dt.float32, kind="ExternalOutput").ap()
    build(nc, *args, out)
    r = run_bass_kernel_spmd(nc, [arrays], core_ids=[0])
    return r.results[0]["outT"].reshape(1, D, SEQ).transpose(0, 2, 1)
```
